# Optimizing a Trainium2 kernel written in Bass

```python
import math
import jax, jax.numpy as jnp
from jax import lax
import numpy as np

D_MODEL = 1024
BATCH = 1
SEQ = 1024
DEPTH = 2

N_EVEN = (DEPTH + 1) // 2
N_ODD = DEPTH // 2
DN_ALPHA = (2.0 * DEPTH) ** 0.25
DN_BETA = (8.0 * DEPTH) ** -0.25

RNN_WIDTH = D_MODEL // 2
RNN_HEADS = 8
RNN_HEAD_DIM = RNN_WIDTH // RNN_HEADS
CONV_WIDTH = 4
RG_C = 8.0

MLA_HEADS = 8
MLA_NOPE = 64
MLA_ROPE = 32
MLA_V = 64
MLA_Q_RANK = D_MODEL // 4
MLA_KV_RANK = D_MODEL // 8
MLA_WIDTH = MLA_HEADS * MLA_V
ROPE_THETA = 10000.0
Q_BLOCK = 128

AB_WIDTH = RNN_WIDTH + MLA_WIDTH
AB_IN = RNN_WIDTH + AB_WIDTH + MLA_Q_RANK + MLA_KV_RANK + MLA_ROPE

SSD_INNER = 2 * D_MODEL
SSD_HEAD_DIM = 64
SSD_HEADS = SSD_INNER // SSD_HEAD_DIM
SSD_GROUPS = 4
SSD_STATE = 128
SSD_CHUNK = 128
SSD_CONV_DIM = SSD_INNER + 2 * SSD_GROUPS * SSD_STATE
SSD_IN = SSD_INNER + SSD_CONV_DIM + SSD_HEADS


def _rmsnorm(x, g, eps=1e-6):
    xf = x.astype(jnp.float32)
    y = xf * lax.rsqrt(jnp.mean(xf * xf, axis=-1, keepdims=True) + eps)
    return (y * g.astype(jnp.float32)).astype(x.dtype)

def _layernorm(x, g, b, eps=1e-5):
    xf = x.astype(jnp.float32)
    mu = jnp.mean(xf, axis=-1, keepdims=True)
    xc = xf - mu
    var = jnp.mean(xc * xc, axis=-1, keepdims=True)
    y = xc * lax.rsqrt(var + eps) * g.astype(jnp.float32) + b.astype(jnp.float32)
    return y.astype(x.dtype)

def _causal_conv(x, w, b):
    k_taps = w.shape[0]
    seqlen = x.shape[1]
    xp = jnp.pad(x, ((0, 0), (k_taps - 1, 0), (0, 0)))
    return sum(xp[:, k:k + seqlen] * w[k] for k in range(k_taps)) + b

def _rope(x, cos, sin):
    half = x.shape[-1] // 2
    x1, x2 = x[..., :half], x[..., half:]
    return jnp.concatenate([x1 * cos - x2 * sin, x2 * cos + x1 * sin], axis=-1)

def _rg_lru(x, w_a, b_a, w_x, b_x, lam):
    bsz, seqlen, _ = x.shape
    xh = x.reshape(bsz, seqlen, RNN_HEADS, RNN_HEAD_DIM)
    r = jax.nn.sigmoid(jnp.einsum('bshi,hij->bshj', xh, w_a).reshape(bsz, seqlen, RNN_WIDTH) + b_a)
    i = jax.nn.sigmoid(jnp.einsum('bshi,hij->bshj', xh, w_x).reshape(bsz, seqlen, RNN_WIDTH) + b_x)
    log_a = (-RG_C * r.astype(jnp.float32)) * jax.nn.softplus(-lam.astype(jnp.float32))
    a = jnp.exp(log_a)
    mult = jnp.sqrt(-jnp.expm1(2.0 * log_a))
    u = mult * (i * x).astype(jnp.float32)

    def combine(c1, c2):
        a1, b1 = c1
        a2, b2 = c2
        return a1 * a2, a2 * b1 + b2

    _, h = lax.associative_scan(combine, (a, u), axis=1)
    return h.astype(x.dtype)

def _mla_attention(q_nope, q_rope, k_nope, k_rope, v):
    seqlen = q_nope.shape[1]
    scale = (MLA_NOPE + MLA_ROPE) ** -0.5
    outs = []
    for blk in range(seqlen // Q_BLOCK):
        q0 = blk * Q_BLOCK
        kend = q0 + Q_BLOCK
        s = (jnp.einsum('bqhd,bkhd->bhqk', q_nope[:, q0:kend], k_nope[:, :kend])
             + jnp.einsum('bqhr,bkr->bhqk', q_rope[:, q0:kend], k_rope[:, :kend]))
        s = s.astype(jnp.float32) * scale
        mask = jnp.arange(kend)[None, :] <= (q0 + jnp.arange(Q_BLOCK))[:, None]
        s = jnp.where(mask, s, -jnp.inf)
        p = jax.nn.softmax(s, axis=-1).astype(v.dtype)
        outs.append(jnp.einsum('bhqk,bkhd->bqhd', p, v[:, :kend]))
    return jnp.concatenate(outs, axis=1)

def _rglru_mla_layer(x, cos, sin, w_in, conv_w, conv_b, gate_a_w, gate_a_b, gate_x_w,
                     gate_x_b, lam, q_norm, kv_norm, w_uq, w_ukv, w_out):
    bsz, seqlen, _ = x.shape
    proj = jnp.einsum('bsd,de->bse', x, w_in)
    x_rnn, gate, c_q, c_kv, k_rope = jnp.split(
        proj, [RNN_WIDTH, RNN_WIDTH + AB_WIDTH, RNN_WIDTH + AB_WIDTH + MLA_Q_RANK,
               RNN_WIDTH + AB_WIDTH + MLA_Q_RANK + MLA_KV_RANK], axis=-1)
    x_rnn = _causal_conv(x_rnn, conv_w, conv_b)
    y_rnn = _rg_lru(x_rnn, gate_a_w, gate_a_b, gate_x_w, gate_x_b, lam)
    q = jnp.einsum('bsr,re->bse', _rmsnorm(c_q, q_norm), w_uq)
    q = q.reshape(bsz, seqlen, MLA_HEADS, MLA_NOPE + MLA_ROPE)
    q_nope = q[..., :MLA_NOPE]
    q_rope = _rope(q[..., MLA_NOPE:], cos[:, :, None], sin[:, :, None])
    kv = jnp.einsum('bsr,re->bse', _rmsnorm(c_kv, kv_norm), w_ukv)
    kv = kv.reshape(bsz, seqlen, MLA_HEADS, MLA_NOPE + MLA_V)
    k_nope, v = kv[..., :MLA_NOPE], kv[..., MLA_NOPE:]
    k_rope = _rope(k_rope, cos, sin)
    y_mla = _mla_attention(q_nope, q_rope, k_nope, k_rope, v).reshape(bsz, seqlen, MLA_WIDTH)
    y = jnp.concatenate([y_rnn, y_mla], axis=-1) * jax.nn.silu(gate)
    return jnp.einsum('bse,ed->bsd', y, w_out)

def _ssd_scan(x, dt, a_neg, bm, cm):
    bsz, seqlen, n_heads, p_dim = x.shape
    n_groups, n_state = bm.shape[2], bm.shape[3]
    hpg = n_heads // n_groups
    nc, L = seqlen // SSD_CHUNK, SSD_CHUNK
    xf = (x.astype(jnp.float32) * dt[..., None]).reshape(bsz, nc, L, n_groups, hpg, p_dim)
    a_dt = (dt * a_neg).reshape(bsz, nc, L, n_groups, hpg)
    bc = bm.astype(jnp.float32).reshape(bsz, nc, L, n_groups, n_state)
    cc = cm.astype(jnp.float32).reshape(bsz, nc, L, n_groups, n_state)
    cs = jnp.cumsum(a_dt, axis=2)
    cs_h = jnp.transpose(cs, (0, 1, 3, 4, 2))
    seg = cs_h[..., :, None] - cs_h[..., None, :]
    causal = jnp.tril(jnp.ones((L, L), dtype=bool))
    decay = jnp.where(causal, jnp.exp(jnp.where(causal, seg, 0.0)), 0.0)
    cb = jnp.einsum('bclgn,bcsgn->bcgls', cc, bc)
    y_diag = jnp.einsum('bcghls,bcsghp->bclghp', cb[:, :, :, None] * decay, xf)
    decay_states = jnp.exp(cs[:, :, -1:] - cs)
    states = jnp.einsum('bclgn,bclghp->bcghpn', bc, xf * decay_states[..., None])
    chunk_decay = jnp.exp(cs[:, :, -1])

    def step(h, inp):
        dec, st = inp
        return h * dec[..., None, None] + st, h

    h0 = jnp.zeros((bsz, n_groups, hpg, p_dim, n_state), jnp.float32)
    _, prev = lax.scan(step, h0, (jnp.moveaxis(chunk_decay, 1, 0), jnp.moveaxis(states, 1, 0)))
    prev = jnp.moveaxis(prev, 0, 1)
    y_off = jnp.einsum('bclgn,bcghpn->bclghp', cc, prev) * jnp.exp(cs)[..., None]
    return (y_diag + y_off).reshape(bsz, seqlen, n_heads, p_dim)

def _ssd_layer(x, w_in, conv_w, conv_b, dt_bias, a_log, d_skip, norm_w, w_out):
    bsz, seqlen, _ = x.shape
    proj = jnp.einsum('bsd,de->bse', x, w_in)
    z, xbc, dt = jnp.split(proj, [SSD_INNER, SSD_INNER + SSD_CONV_DIM], axis=-1)
    xbc = jax.nn.silu(_causal_conv(xbc, conv_w, conv_b))
    xs, bm, cm = jnp.split(xbc, [SSD_INNER, SSD_INNER + SSD_GROUPS * SSD_STATE], axis=-1)
    xs = xs.reshape(bsz, seqlen, SSD_HEADS, SSD_HEAD_DIM)
    bm = bm.reshape(bsz, seqlen, SSD_GROUPS, SSD_STATE)
    cm = cm.reshape(bsz, seqlen, SSD_GROUPS, SSD_STATE)
    dt = jax.nn.softplus(dt.astype(jnp.float32) + dt_bias.astype(jnp.float32))
    a_neg = -jnp.exp(a_log.astype(jnp.float32))
    y = _ssd_scan(xs, dt, a_neg, bm, cm) + d_skip.astype(jnp.float32)[:, None] * xs.astype(jnp.float32)
    y = y.reshape(bsz, seqlen, SSD_INNER) * jax.nn.silu(z.astype(jnp.float32))
    yg = y.reshape(bsz, seqlen, SSD_GROUPS, SSD_INNER // SSD_GROUPS)
    yg = yg * lax.rsqrt(jnp.mean(yg * yg, axis=-1, keepdims=True) + 1e-6)
    y = (yg.reshape(bsz, seqlen, SSD_INNER) * norm_w.astype(jnp.float32)).astype(x.dtype)
    return jnp.einsum('bse,ed->bsd', y, w_out)

def first_inputs(seed: int = 0) -> dict:
    key = jax.random.key(seed)
    ks = jax.random.split(key, 32)
    f32 = jnp.float32
    nrm = lambda k, shape, s: jax.random.normal(k, shape, f32) * s

    x = jax.random.normal(ks[0], (BATCH, SEQ, D_MODEL), f32)
    offset = jax.random.randint(ks[1], (BATCH, 1), 0, 1024, dtype=jnp.int32)
    positions = offset + jnp.arange(SEQ, dtype=jnp.int32)[None, :]

    ab_w_in = nrm(ks[2], (N_EVEN, D_MODEL, AB_IN), D_MODEL ** -0.5)
    ab_conv_w = nrm(ks[3], (N_EVEN, CONV_WIDTH, RNN_WIDTH), CONV_WIDTH ** -0.5)
    ab_conv_b = nrm(ks[4], (N_EVEN, RNN_WIDTH), 0.02)
    ab_gate_a_w = nrm(ks[5], (N_EVEN, RNN_HEADS, RNN_HEAD_DIM, RNN_HEAD_DIM), RNN_HEAD_DIM ** -0.5)
    ab_gate_a_b = nrm(ks[6], (N_EVEN, RNN_WIDTH), 0.1)
    ab_gate_x_w = nrm(ks[7], (N_EVEN, RNN_HEADS, RNN_HEAD_DIM, RNN_HEAD_DIM), RNN_HEAD_DIM ** -0.5)
    ab_gate_x_b = nrm(ks[8], (N_EVEN, RNN_WIDTH), 0.1)
    u = jax.random.uniform(ks[9], (N_EVEN, RNN_WIDTH), f32, 0.9, 0.999)
    a0 = u ** (1.0 / RG_C)
    ab_lambda = jnp.log(a0) - jnp.log1p(-a0)
    mla_q_norm = 1.0 + nrm(ks[10], (N_EVEN, MLA_Q_RANK), 0.05)
    mla_kv_norm = 1.0 + nrm(ks[11], (N_EVEN, MLA_KV_RANK), 0.05)
    mla_w_uq = nrm(ks[12], (N_EVEN, MLA_Q_RANK, MLA_HEADS * (MLA_NOPE + MLA_ROPE)), MLA_Q_RANK ** -0.5)
    mla_w_ukv = nrm(ks[13], (N_EVEN, MLA_KV_RANK, MLA_HEADS * (MLA_NOPE + MLA_V)), MLA_KV_RANK ** -0.5)
    ab_w_out = nrm(ks[14], (N_EVEN, AB_WIDTH, D_MODEL), DN_BETA * math.sqrt(2.0 / (AB_WIDTH + D_MODEL)))
    ab_ln_g = 1.0 + nrm(ks[15], (N_EVEN, D_MODEL), 0.05)
    ab_ln_b = nrm(ks[16], (N_EVEN, D_MODEL), 0.02)

    ssd_w_in = nrm(ks[17], (N_ODD, D_MODEL, SSD_IN), D_MODEL ** -0.5)
    ssd_conv_w = nrm(ks[18], (N_ODD, CONV_WIDTH, SSD_CONV_DIM), CONV_WIDTH ** -0.5)
    ssd_conv_b = nrm(ks[19], (N_ODD, SSD_CONV_DIM), 0.02)
    dt0 = jnp.exp(jax.random.uniform(ks[20], (N_ODD, SSD_HEADS), f32, math.log(1e-3), math.log(1e-1)))
    ssd_dt_bias = dt0 + jnp.log(-jnp.expm1(-dt0))
    ssd_a_log = jnp.log(jax.random.uniform(ks[21], (N_ODD, SSD_HEADS), f32, 1.0, 16.0))
    ssd_d = 1.0 + nrm(ks[22], (N_ODD, SSD_HEADS), 0.1)
    ssd_norm = 1.0 + nrm(ks[23], (N_ODD, SSD_INNER), 0.05)
    ssd_w_out = nrm(ks[24], (N_ODD, SSD_INNER, D_MODEL), DN_BETA * math.sqrt(2.0 / (SSD_INNER + D_MODEL)))
    ssd_ln_g = 1.0 + nrm(ks[25], (N_ODD, D_MODEL), 0.05)
    ssd_ln_b = nrm(ks[26], (N_ODD, D_MODEL), 0.02)

    return {"x": x, "positions": positions,
            "ab_w_in": ab_w_in, "ab_conv_w": ab_conv_w, "ab_conv_b": ab_conv_b,
            "ab_gate_a_w": ab_gate_a_w, "ab_gate_a_b": ab_gate_a_b,
            "ab_gate_x_w": ab_gate_x_w, "ab_gate_x_b": ab_gate_x_b,
            "ab_lambda": ab_lambda, "mla_q_norm": mla_q_norm, "mla_kv_norm": mla_kv_norm,
            "mla_w_uq": mla_w_uq, "mla_w_ukv": mla_w_ukv, "ab_w_out": ab_w_out,
            "ab_ln_g": ab_ln_g, "ab_ln_b": ab_ln_b,
            "ssd_w_in": ssd_w_in, "ssd_conv_w": ssd_conv_w, "ssd_conv_b": ssd_conv_b,
            "ssd_dt_bias": ssd_dt_bias, "ssd_a_log": ssd_a_log, "ssd_d": ssd_d,
            "ssd_norm": ssd_norm, "ssd_w_out": ssd_w_out,
            "ssd_ln_g": ssd_ln_g, "ssd_ln_b": ssd_ln_b}

def first_block(x, positions, ab_w_in, ab_conv_w, ab_conv_b, ab_gate_a_w, ab_gate_a_b,
              ab_gate_x_w, ab_gate_x_b, ab_lambda, mla_q_norm, mla_kv_norm, mla_w_uq,
              mla_w_ukv, ab_w_out, ab_ln_g, ab_ln_b, ssd_w_in, ssd_conv_w, ssd_conv_b,
              ssd_dt_bias, ssd_a_log, ssd_d, ssd_norm, ssd_w_out, ssd_ln_g, ssd_ln_b):
    inv_freq = ROPE_THETA ** (-jnp.arange(0, MLA_ROPE, 2, dtype=jnp.float32) / MLA_ROPE)
    ang = positions.astype(jnp.float32)[..., None] * inv_freq
    cos = jnp.cos(ang).astype(x.dtype)
    sin = jnp.sin(ang).astype(x.dtype)
    for layer in range(DEPTH):
        j = layer // 2
        if layer % 2 == 0:
            y = _rglru_mla_layer(x, cos, sin, ab_w_in[j], ab_conv_w[j], ab_conv_b[j],
                                 ab_gate_a_w[j], ab_gate_a_b[j], ab_gate_x_w[j], ab_gate_x_b[j],
                                 ab_lambda[j], mla_q_norm[j], mla_kv_norm[j], mla_w_uq[j],
                                 mla_w_ukv[j], ab_w_out[j])
            x = _layernorm(DN_ALPHA * x + y, ab_ln_g[j], ab_ln_b[j])
        else:
            y = _ssd_layer(x, ssd_w_in[j], ssd_conv_w[j], ssd_conv_b[j], ssd_dt_bias[j],
                           ssd_a_log[j], ssd_d[j], ssd_norm[j], ssd_w_out[j])
            x = _layernorm(DN_ALPHA * x + y, ssd_ln_g[j], ssd_ln_b[j])
    return x


DEPTH_2 = 1

HEAD_DIM = 64
W_CONV = D_MODEL // 2
W_ATTN = D_MODEL - W_CONV
N_CONV_GROUPS = W_CONV // HEAD_DIM
N_ATTN_HEADS = W_ATTN // HEAD_DIM
CONV_K = 3
D_FF = 4 * D_MODEL
PLE_DIM = 256
EPS = 1e-6
IN_COLS = 3 * W_CONV + 3 * W_ATTN


def rmsnorm(x, g):
    xf = x.astype(jnp.float32)
    y = xf * lax.rsqrt(jnp.mean(xf * xf, axis=-1, keepdims=True) + EPS)
    return (y * g.astype(jnp.float32)).astype(x.dtype)

def head_rmsnorm(y, g):
    b, s, w = y.shape
    yf = y.astype(jnp.float32).reshape(b, s, w // HEAD_DIM, HEAD_DIM)
    yf = yf * lax.rsqrt(jnp.mean(yf * yf, axis=-1, keepdims=True) + EPS)
    return (yf.reshape(b, s, w) * g.astype(jnp.float32)).astype(y.dtype)

def short_gated_conv(b_gate, c_gate, u, w_conv):
    v = c_gate * u
    y = lax.conv_general_dilated(
        v, w_conv[:, None, :].astype(v.dtype),
        window_strides=(1,), padding=[(CONV_K - 1, 0)],
        dimension_numbers=('NWC', 'WIO', 'NWC'),
        feature_group_count=v.shape[-1])
    return b_gate * y

def stick_breaking_attention(q, k, v):
    b, h, s, dh = q.shape
    n_blk = s // Q_BLOCK
    scale = dh ** -0.5
    qb = q.reshape(b, h, n_blk, Q_BLOCK, dh).transpose(2, 0, 1, 3, 4)
    kf = k.astype(jnp.float32)
    vf = v.astype(jnp.float32)
    key_pos = jnp.arange(s)

    def one_block(args):
        qi, blk = args
        z = jnp.einsum('bhqd,bhkd->bhqk', qi.astype(jnp.float32), kf) * scale
        q_pos = blk * Q_BLOCK + jnp.arange(Q_BLOCK)
        mask = key_pos[None, :] < q_pos[:, None]
        log_keep = jnp.where(mask, jax.nn.log_sigmoid(-z), 0.0)
        suffix = lax.cumsum(log_keep, axis=3, reverse=True) - log_keep
        a = jnp.where(mask, jnp.exp(jax.nn.log_sigmoid(z) + suffix), 0.0)
        return jnp.einsum('bhqk,bhkd->bhqd', a, vf)

    out = lax.map(one_block, (qb, jnp.arange(n_blk)))
    return out.transpose(1, 2, 0, 3, 4).reshape(b, h, s, dh).astype(q.dtype)

def second_inputs(seed: int = 0) -> dict:
    key = jax.random.key(seed)
    ks = jax.random.split(key, 20)
    f32 = jnp.float32

    def nrm(k, shape, fan_in):
        return jax.random.normal(k, shape, f32) * (fan_in ** -0.5)

    def gain(k, shape):
        return 1.0 + 0.02 * jax.random.normal(k, shape, f32)

    return {
        "x": jax.random.normal(ks[0], (BATCH, SEQ, D_MODEL), f32),
        "p": jax.random.normal(ks[1], (DEPTH_2, BATCH, SEQ, PLE_DIM), f32),
        "g_mix": gain(ks[2], (DEPTH_2, D_MODEL)),
        "w_in": nrm(ks[3], (DEPTH_2, D_MODEL, IN_COLS), D_MODEL),
        "conv_w": nrm(ks[4], (DEPTH_2, CONV_K, W_CONV), CONV_K),
        "g_conv_out": gain(ks[5], (DEPTH_2, W_CONV)),
        "g_attn_out": gain(ks[6], (DEPTH_2, W_ATTN)),
        "w_out": nrm(ks[7], (DEPTH_2, W_CONV + W_ATTN, D_MODEL), W_CONV + W_ATTN),
        "g_mlp": gain(ks[8], (DEPTH_2, D_MODEL)),
        "w_up": nrm(ks[9], (DEPTH_2, D_MODEL, D_FF), D_MODEL),
        "w_down": nrm(ks[10], (DEPTH_2, D_FF, D_MODEL), D_FF),
        "g_ple": gain(ks[11], (DEPTH_2, D_MODEL)),
        "w_ple_gate": nrm(ks[12], (DEPTH_2, D_MODEL, D_MODEL), D_MODEL),
        "w_ple_proj": nrm(ks[13], (DEPTH_2, PLE_DIM, D_MODEL), PLE_DIM),
        "g_final": gain(ks[14], (D_MODEL,)),
    }

def second_block(x, p, g_mix, w_in, conv_w, g_conv_out, g_attn_out, w_out, g_mlp, w_up, w_down,
              g_ple, w_ple_gate, w_ple_proj, g_final):
    b, s, _ = x.shape
    splits = [W_CONV, 2 * W_CONV, 3 * W_CONV, 3 * W_CONV + W_ATTN, 3 * W_CONV + 2 * W_ATTN]
    h = x
    for i in range(DEPTH_2):
        a = rmsnorm(h, g_mix[i])
        proj = a @ w_in[i]
        cb, cc, cu, q, k, v = jnp.split(proj, splits, axis=-1)
        conv_out = head_rmsnorm(short_gated_conv(cb, cc, cu, conv_w[i]), g_conv_out[i])
        to_heads = lambda t: t.reshape(b, s, N_ATTN_HEADS, HEAD_DIM).transpose(0, 2, 1, 3)
        attn = stick_breaking_attention(to_heads(q), to_heads(k), to_heads(v))
        attn = head_rmsnorm(attn.transpose(0, 2, 1, 3).reshape(b, s, W_ATTN), g_attn_out[i])
        h = h + jnp.concatenate([conv_out, attn], axis=-1) @ w_out[i]
        m = rmsnorm(h, g_mlp[i])
        h = h + jnp.square(jax.nn.relu(m @ w_up[i])) @ w_down[i]
        gate = jax.nn.sigmoid(rmsnorm(h, g_ple[i]) @ w_ple_gate[i])
        h = h + gate * (p[i] @ w_ple_proj[i])
    return rmsnorm(h, g_final)


_first_inputs = second_inputs


def second_inputs(seed=0):
    import zlib

    import numpy as np

    out = dict(_first_inputs(seed))
    spreads = {}
    factors = {'g_conv_out': 5.269, 'g_attn_out': 5.317, 'g_mlp': 4.081, 'g_ple': 8.0, 'g_final': 2.88}
    for name, (base, spread) in spreads.items():
        noise = np.random.default_rng([zlib.crc32(name.encode()), seed]).standard_normal(out[name].shape)
        drawn = base * np.exp(spread * noise) if base else spread * noise
        out[name] = __import__('jax').numpy.asarray(drawn.astype(out[name].dtype))
    for name, factor in factors.items():
        out[name] = (out[name] * factor).astype(out[name].dtype)
    return out


_narrow_inputs = second_inputs


def second_inputs(seed=0):

    out = dict(_narrow_inputs(seed))
    wider = {'g_conv_out': 3.87, 'g_attn_out': 3.86, 'g_ple': 12.0, 'g_final': 3.25}
    for name, times in wider.items():
        mean = out[name].mean()
        out[name] = (mean + times * (out[name] - mean)).astype(out[name].dtype)
    return out


def setup_inputs(seed=0):
    out = dict(first_inputs(seed))
    for name, value in second_inputs(seed + 1).items():
        if name != "x":
            out[name + "_2"] = value
    return out


def reference(
    x, positions, ab_w_in, ab_conv_w, ab_conv_b, ab_gate_a_w, ab_gate_a_b, ab_gate_x_w,
    ab_gate_x_b, ab_lambda, mla_q_norm, mla_kv_norm, mla_w_uq, mla_w_ukv, ab_w_out, ab_ln_g,
    ab_ln_b, ssd_w_in, ssd_conv_w, ssd_conv_b, ssd_dt_bias, ssd_a_log, ssd_d, ssd_norm,
    ssd_w_out, ssd_ln_g, ssd_ln_b, p_2, g_mix_2, w_in_2, conv_w_2, g_conv_out_2, g_attn_out_2,
    w_out_2, g_mlp_2, w_up_2, w_down_2, g_ple_2, w_ple_gate_2, w_ple_proj_2, g_final_2,
):
    x = first_block(
        x, positions, ab_w_in, ab_conv_w, ab_conv_b, ab_gate_a_w, ab_gate_a_b, ab_gate_x_w,
        ab_gate_x_b, ab_lambda, mla_q_norm, mla_kv_norm, mla_w_uq, mla_w_ukv, ab_w_out, ab_ln_g,
        ab_ln_b, ssd_w_in, ssd_conv_w, ssd_conv_b, ssd_dt_bias, ssd_a_log, ssd_d, ssd_norm,
        ssd_w_out, ssd_ln_g, ssd_ln_b,
    )
    return second_block(
        x, p_2, g_mix_2, w_in_2, conv_w_2, g_conv_out_2, g_attn_out_2, w_out_2, g_mlp_2, w_up_2,
        w_down_2, g_ple_2, w_ple_gate_2, w_ple_proj_2, g_final_2,
    )


_drawn_inputs = setup_inputs


def setup_inputs(seed=0):
    import zlib

    import numpy as np

    out = dict(_drawn_inputs(seed))
    spreads = {}
    factors = {'ab_gate_a_b': 8.0,
     'ab_gate_x_b': 8.0,
     'mla_q_norm': 8.0,
     'mla_kv_norm': 8.0,
     'ssd_conv_b': 3.063,
     'g_ple_2': 39.678,
     'ab_conv_b': 2.729}
    for name, (base, spread) in spreads.items():
        noise = np.random.default_rng([zlib.crc32(name.encode()), seed]).standard_normal(out[name].shape)
        drawn = base * np.exp(spread * noise) if base else spread * noise
        out[name] = __import__('jax').numpy.asarray(drawn.astype(out[name].dtype))
    for name, factor in factors.items():
        out[name] = (out[name] * factor).astype(out[name].dtype)
    return out
```

```python
import concourse.bass as bass
from concourse import mybir
from contextlib import ExitStack
import numpy as np

F32 = mybir.dt.float32
F32R = mybir.dt.float32r
BF16 = mybir.dt.bfloat16
I32 = mybir.dt.int32
ALU = mybir.AluOpType
ACT = mybir.ActivationFunctionType
AX = mybir.AxisListType

P = 128
TOK = 1024
HB = 512
D = 1024
KT = D // P
ALPHA = (2.0 * 2) ** 0.25
RNN_T = 4
RG_C = 8.0
MLA_H = 8
NOPE, ROPE, VDIM = 64, 32, 64
MLA_SCALE = float(NOPE + ROPE) ** -0.5
GROUPS, HPG, PDIM = 4, 8, 64
CHUNKS = TOK // P
SSD_HEADS = GROUPS * HPG
SB_SCALE = 64.0 ** -0.5
FFN_BLOCKS = 8
NEG = -1.0e30

N_RNN, N_GATES, N_GATE, N_LAT, N_HEADS, N_OUT_A = 0, 4, 5, 13, 17, 25
N_DT = 33
N_SSD = 34
SSD_SLABS = 14
N_CORE = N_SSD + 7
N_IN2 = N_SSD + GROUPS * SSD_SLABS
N_OUT2 = N_IN2 + 24
N_FFN = N_OUT2 + 8
N_PLE = N_FFN + FFN_BLOCKS * 8
NSLAB = N_PLE + 10

VEC = {}
_at = 0
for _name, _n in [("conv_w", 16), ("conv_b", 4), ("ba", 4), ("bx", 4), ("lam", 4), ("qn", 2), ("kvn", 1),
                  ("ln1_g", 8), ("ln1_b", 8), ("sc_w", 96), ("sc_b", 24), ("ssd_d", 16), ("ssd_n", 16),
                  ("ln2_g", 8), ("ln2_b", 8), ("g_mix", 8), ("c2_w", 12), ("g_co", 4), ("g_at", 4),
                  ("g_mlp", 8), ("g_ple", 8), ("g_fin", 8), ("trig", 3)]:
    VEC[_name] = _at
    _at += _n
NVEC = _at
C_ID, C_AFTER, C_UPTO, C_ONES, C_BLK, C_NEGQ, C_NEGK, C_NOTLATER, C_NEGS = range(9)
NCONST = 9
SB_UNITS = [(hf, j) for hf in range(2) for j in range(4 * hf + 3, -1, -1)]
NU = len(SB_UNITS)
N_SB = N_IN2 + 12
DT_STEPS = 23
TWO_PI_PARTS = (6.28125, 0.0019350051879882812, 3.019916050561733e-07)


MAX_STEPS = {5: (0, 1), 6: (2, 3), 7: (4,), 8: (5,), 9: (6,), 10: (7,)}


class Tally:

    def __init__(self, eng, sem, base=0):
        self.eng, self.sem, self.n, self.start = eng, sem, base, 0

    def __call__(self, ins):
        ins.then_inc(self.sem, 1)
        self.n = self.n + 1

    def wait(self):
        self.eng.wait_ge(self.sem, self.n)

    def loop(self, i, per):
        self.start, self.per = self.n, per
        self.n = i * per + self.start

    def end(self, times):
        self.n = self.start + self.per * times


def program(nc, x_t, pos, w, vec, rows, consts, p_t, out):
    ctx = ExitStack()
    with ctx:
        base = [(nc.sbuf_base + 31) // 32 * 32]

        def place(at, name, shape, dt):
            n = int(np.prod(shape[1:])) * (2 if dt == BF16 else 4)
            t = nc.alloc_sbuf_tensor_at(name, shape, dt, offset=at)
            return t, at + (n + 31) // 32 * 32

        def sb(name, shape, dt=F32):
            t, base[0] = place(base[0], name, shape, dt)
            return t

        def sem(name):
            return ctx.enter_context(nc.semaphore(name))

        def region(specs):
            at, got = base[0], []
            for name, shape, dt in specs:
                t, at = place(at, name, shape, dt)
                got.append(t)
            assert at <= nc.sbuf_usable_end, (at, nc.sbuf_usable_end)
            return got, at

        w_stage = sb("w_stage", [P, 2, 8, P])
        w_hi = sb("w_hi", [P, 2, 8, P], F32R)
        w_lo = sb("w_lo", [P, 2, 8, P], F32R)
        H = sb("H", [P, KT, TOK])
        XH = sb("XH", [P, KT, TOK], F32R)
        XL = sb("XL", [P, KT, TOK], F32R)
        VC = sb("VC", [P, NVEC])
        CN = sb("CN", [P, NCONST, P])
        RW = sb("RW", [P, 96])
        ident_b = sb("ident_b", [P, P], BF16)
        negq_b = sb("negq_b", [P, P], BF16)
        negk_b = sb("negk_b", [P, P], BF16)
        SM = sb("SM", [P, 10, 8])
        EPS5, EPS6 = SM[:, 0, 6:7], SM[:, 0, 7:8]
        XH_f, XL_f = XH[:, :, :].bitcast(F32), XL[:, :, :].bitcast(F32)

        PS = ctx.enter_context(nc.psum_tensor("PS", [P, 8, HB], F32))

        def pair(p):
            return PS[:, 2 * p:2 * p + 2, :]

        def flat(p):
            return pair(p).rearrange("p b t -> p (b t)")

        def col(name, j=0, n=1):
            return VC[:, VEC[name] + j:VEC[name] + j + n]

        (XCH, XCL, R, I_, A_, T_), _ = region([
            ("rnn_conv_hi", [P, RNN_T, TOK], F32R), ("rnn_conv_lo", [P, RNN_T, TOK], F32R),
            ("rnn_r", [P, RNN_T, TOK], F32), ("rnn_i", [P, RNN_T, TOK], F32),
            ("rnn_a", [P, 1, TOK], F32), ("rnn_t", [P, 1, TOK], F32)])
        (CQH, CQL, CKH, CKL, TRIG, K_, V_, MX, Q_), at = region([
            ("cq_hi", [P, 2, TOK], F32R), ("cq_lo", [P, 2, TOK], F32R), ("ckv_hi", [P, TOK], F32R),
            ("ckv_lo", [P, TOK], F32R), ("trig", [P, TOK], F32), ("mla_k", [P, 2, TOK], F32),
            ("mla_v", [P, 2, KT, P], F32), ("mla_mx", [P, 2, 8], F32), ("mla_q", [P, 2, TOK], F32)])
        PT, at1 = place(at, "mla_p", [P, 3, HB], F32)
        RT, at1 = place(at1, "mla_rope", [P, 2, TOK], F32)
        RC, at1 = place(at1, "mla_rc", [P, 2, HB], F32)
        VR, at1 = place(at1, "mla_v_rows", [P, TOK], F32)
        CQ, at2 = place(at, "cq", [P, 3, TOK], F32)
        SQ, at2 = place(at2, "cq_sq", [P, 1, TOK], F32)
        assert max(at1, at2) <= nc.sbuf_usable_end, (at1, at2)
        AN, _ = place(at, "angle", [P, 2, TOK], F32)

        (XR, TN, SQN, MU, RS), _ = region([
            ("x_again", [P, 2, TOK], F32), ("norm_t", [P, 2, TOK], F32), ("norm_sq", [P, 2, TOK], F32),
            ("norm_mu", [P, TOK], F32), ("norm_rs", [P, TOK], F32)])

        at = base[0]
        XS, at = place(at, "ssd_x", [P, 4, TOK], F32)
        YH, _ = place(base[0], "ssd_y_hi", [P, 4, TOK], F32R)
        YL, _ = place(at, "ssd_y_lo", [P, 4, TOK], F32R)
        Z, at = place(at, "ssd_z", [P, 4, TOK], F32)
        BT, at = place(at, "ssd_b", [P, TOK], F32)
        CT, at = place(at, "ssd_c", [P, TOK], F32)
        DTS, at = place(at, "ssd_dt", [P, 6, CHUNKS * SSD_HEADS], F32)
        AV, at = place(at, "ssd_a_upto", [P, HPG, P], F32)
        E, at = place(at, "ssd_decay", [P, 2, HPG, P], F32)
        CV, _ = place(at, "ssd_conv", [P, 2, TOK], F32)
        XF, at = place(at, "ssd_xdt", [P, 2, HB], F32)
        XFD, at = place(at, "ssd_xdt_decayed", [P, 2, HB], F32)
        BK, at = place(at, "ssd_b_rows", [P, 2, P], F32)
        CB, at = place(at, "ssd_cb", [P, P], F32)
        ST, at = place(at, "ssd_state", [P, HB], F32)
        YR, at = place(at, "ssd_y_rows", [P, 2, HB], F32)
        assert at <= nc.sbuf_usable_end, at
        SUM2 = YR[:, :, :].rearrange("p a b -> p (a b)")
        DTR = E[:, 1, :, :].rearrange("p h l -> p (h l)")
        DT, ADT, DS, ECS, DEC = (DTS[:, q, :].rearrange("p (c h) -> p c h", h=SSD_HEADS) for q in range(5))

        (CONV, ATT, QH, KH, VT, VH, SB_L, SB_P, SB_A), at = region([
            ("conv_out", [P, 4, TOK], F32), ("attn_out", [P, 4, TOK], F32), ("sb_q", [P, TOK], F32), ("sb_k", [P, TOK], F32),
            ("sb_v_t", [P, TOK], F32), ("sb_v", [P, KT, P], F32), ("sb_log", [P, 2, 2, HB], F32),
            ("sb_softplus", [P, 3, 2, HB], F32), ("sb_a", [P, 3, 2, HB], F32)])
        at = base[0] + 48 * 1024
        HQ, at = place(at, "head_sq", [P, 2, TOK], F32)
        HR, at = place(at, "head_rs", [P, 2, TOK], F32)
        HT, at = place(at, "head_t", [P, 2, TOK], F32)
        CC = SB_P[:, 0, :, :].rearrange("p a b -> p (a b)")
        CU = SB_P[:, 1, :, :].rearrange("p a b -> p (a b)")
        (FT, UH, UL), _ = region([("ffn_t", [P, 2, TOK], F32), ("ffn_u_hi", [P, 2, 4, TOK], F32R), ("ffn_u_lo", [P, 2, 4, TOK], F32R)])
        PJ, at = place(base[0] + 32 * 1024, "ple_proj", [P, KT, TOK], F32)
        PH, at = place(at, "ple_p_hi", [P, 2, TOK], F32R)
        PL, at = place(at, "ple_p_lo", [P, 2, TOK], F32R)
        assert at <= nc.sbuf_usable_end, at

        s_const = sem("const_loaded")
        s_dtt = sem("dt_turned")
        s_zs = sem("ssd_z_silu")
        s_hp = sem("mla_head_projected")
        s_w_loaded = [sem("w_loaded_even"), sem("w_loaded_odd")]
        s_w_hi = sem("w_hi_made")
        s_w_ready = sem("w_ready")
        s_slab = sem("slab_done")
        s_evac = [sem("evac_even"), sem("evac_odd")]
        s_st_out = [sem("out_stored_even"), sem("out_stored_odd")]
        s_dg = sem("sb_diagonal_steps")

        block = ctx.enter_context(nc.Block())

        s_x = [sem(f"x_loaded{j}") for j in range(4)]
        s_setup = sem("setup_dve")
        s_xhi = sem("x_hi_made")
        s_xlo = sem("x_split")
        s_conv = sem("rnn_conv_steps")
        s_chi = sem("rnn_conv_hi_made")
        s_clo = sem("rnn_conv_split")
        s_gmm = sem("rnn_gate_products")
        s_sig = sem("rnn_sigmoids")
        s_lam = sem("lambda_steps_dve")
        s_lama = sem("lambda_steps_act")
        s_ra = sem("rnn_decay_act")
        s_rd = sem("rnn_steps_dve")
        s_yr = sem("rnn_gated")
        s_pos = sem("positions_loaded")
        s_tr = sem("trig_steps")
        s_sin = sem("trig_ready")
        s_sq = sem("latent_squares")
        s_ss = sem("latent_square_sums")
        s_lat = sem("latent_steps_dve")
        s_rs = sem("latent_roots")
        s_lhi = sem("latent_hi_made")
        s_llo = sem("latent_split")
        s_kr = sem("key_rope_steps")
        s_qkv = sem("mla_qkv_copied")
        s_rope = sem("mla_rope_steps")
        s_s = sem("mla_score_rows")
        s_mx = sem("mla_row_maxima")
        s_row = sem("mla_maxima_across")
        s_neg = sem("mla_maxima_in_queries")
        s_st = sem("mla_score_tiles")
        s_e = sem("mla_exponentials")
        s_pv = sem("mla_value_products")
        s_y = sem("mla_output_steps")
        s_yhi = sem("gated_hi_made")
        s_ylo = sem("gated_split")
        s_xr = [sem("x_again_even"), sem("x_again_odd")]

        norm_parts = {k: sem(f"norm_{v}") for k, v in dict(
            c="centre_steps", cs="centre_sum", sq="squares", ss="square_sums", v="logarithm", rs="root",
            t="scaled", h="shifted", hi="hi_made", lo="split").items()}
        norm_counts = dict.fromkeys(norm_parts, 0)

        class Part:

            def __init__(self, sem, base):
                self.sem, self.base = sem, base

            def wait(self, eng, n):
                eng.wait_ge(self.sem, self.base + n)

        def norm_sems(center=False, bias=False, split=True):
            parts = {k: Part(norm_parts[k], norm_counts[k]) for k in norm_parts}
            for k, n in dict(c=16 * center, cs=center, sq=8, ss=8, v=1, rs=1, t=8, h=8 * bias, hi=8 * split, lo=8 * split).items():
                norm_counts[k] += n
            return parts

        ln1 = norm_sems(True, True)
        ln2 = norm_sems(True, True, False)
        mix = norm_sems()
        mlp = norm_sems()
        ple = norm_sems()
        fin = norm_sems(split=False)
        s_cc = sem("conv2_steps")
        s_vt = sem("sb_v_turned")
        s_vc = sem("sb_v_copied")
        s_z = sem("sb_scores")
        s_al = sem("sb_log_steps")
        s_sp = sem("sb_softplus_made")
        s_ls = sem("sb_log_sigmoid_made")
        s_su = sem("sb_suffix_sums")
        s_d = sem("sb_log_weights")
        s_w = sem("sb_weights")
        s_o = sem("sb_value_products")
        s_at = sem("sb_output_copied")
        s_hq = sem("head_squares")
        s_hs = sem("head_square_sums")
        s_hv = sem("head_variance_steps")
        s_hr = sem("head_roots")
        s_ht = sem("head_scaled")
        s_hh = sem("head_hi_made")
        s_hl = sem("head_split")
        s_ff = sem("ffn_squared")
        s_fh = sem("ffn_hi_made")
        s_fl = sem("ffn_split")
        s_fo = sem("ffn_down_half_done")
        s_fe = sem("ffn_down_even_added")
        s_pl = sem("ple_p_loaded")
        s_ph = sem("ple_p_hi_made")
        s_pw = sem("ple_p_split")
        s_pm = sem("ple_proj_products")
        s_pj = sem("ple_proj_copied")
        s_sg = sem("ple_gated")
        s_h3 = sem("ple_added")
        s_dt = sem("dt_steps_dve")
        s_dta = sem("dt_steps_act")
        s_dtp = sem("dt_sums")
        s_cv = sem("ssd_conv_steps")
        s_cs = sem("ssd_conv_silus")
        s_av = sem("ssd_a_upto_made")
        s_cb = sem("ssd_chunk_turned")
        s_seg = sem("ssd_segments")
        s_ex = sem("ssd_decays")
        s_bk = sem("ssd_b_rows_copied")
        s_a = sem("ssd_chunk_inputs")
        s_m = sem("ssd_mixed")
        s_core = sem("ssd_chunk_products")
        s_b = sem("ssd_chunk_steps")
        s_yt = sem("ssd_y_turned")
        s_c = sem("ssd_skip_steps")
        s_g = sem("ssd_gated")
        s_gs = sem("ssd_gated_squares")
        s_gss = sem("ssd_square_sums")
        s_gv = sem("ssd_variance_steps")
        s_gr = sem("ssd_root")
        s_gt = sem("ssd_scaled")
        s_gh = sem("ssd_hi_made")
        s_gl = sem("ssd_split")
        s_oe = sem("ssd_out_even")
        s_oh = sem("ssd_out_half_done")

        @block.sync
        def _(sp):
            def fetch(n, slot):
                sp.dma_start(w_stage[:, slot, :, :].rearrange("p a b -> p (a b)"),
                             w[bass.ds(n, 1), :, :].rearrange("o p f -> (o p) f")).then_inc(s_w_loaded[slot], 16)

            fetch(0, 0)
            fetch(1, 1)
            with sp.Fori(1, NSLAB // 2) as i:
                for slot in range(2):
                    sp.wait_ge(s_w_ready, 2 * i + (slot - 1))
                    fetch(2 * i + slot, slot)

        @block.gpsimd
        def _(pool):
            def split(n, slot, loaded, hi_count):
                pool.wait_ge(s_w_loaded[slot], loaded)
                nc.gpsimd.tensor_tensor(w_hi[:, slot, :, :], w_stage[:, slot, :, :],
                                        CN[:, C_ONES, :].unsqueeze(1).to_broadcast([P, 8, P]), ALU.mult).then_inc(s_w_hi, 1)
                pool.wait_ge(s_w_hi, hi_count)
                nc.gpsimd.tensor_tensor(w_lo[:, slot, :, :], w_stage[:, slot, :, :],
                                        w_hi[:, slot, :, :].bitcast(F32), ALU.subtract).then_inc(s_w_ready, 1)

            pool.wait_ge(s_const, 48)
            split(0, 0, 16, 1)
            split(1, 1, 16, 2)
            with pool.Fori(1, NSLAB // 2) as i:
                for slot in range(2):
                    pool.wait_ge(s_slab, 2 * i + (slot - 1))
                    split(2 * i + slot, slot, 16 * i + 16, 2 * i + (slot + 1))

        class Tiles:

            def __init__(self, n0):
                self.n0 = n0

            def wait(self, eng, k):
                n = self.n0 + k
                eng.wait_ge(s_evac[n % 2], n // 2 + 1)

        class Done(Tiles):

            def __init__(self):
                pass

            def wait(self, eng, k):
                for n in (N_PLE - 2, N_PLE - 1):
                    eng.wait_ge(s_evac[n % 2], n // 2 + 1)

        @block.tensor
        def _(pe):
            def product(outs, n, hi, lo, tiles=range(8), first=0, whole=None, ready=None):
                whole = whole or tiles
                slot = n % 2
                for k in tiles:
                    if ready is not None:
                        pe.wait_ge(ready[0], ready[1] + (k - first + 1))
                    for wt, acts in ((w_hi, (hi, lo)), (w_lo, (hi,))):
                        for a in acts:
                            for half in range(2):
                                mm = nc.tensor.matmul(
                                    outs[:, half, :], wt[:, slot, k, :], a[:, k - first, half * HB:(half + 1) * HB],
                                    start=(k == whole[0] and wt is w_hi and a is hi),
                                    stop=(k == whole[-1] and wt is w_lo))
                return mm

            def take(n, dyn=0, half_dyn=0):
                pe.wait_ge(s_w_ready, dyn + (n + 1))
                if n >= 2:
                    pe.wait_ge(s_evac[n % 2], half_dyn + n // 2)

            for n in range(4):
                take(n)
                if n == 0:
                    for k in range(8):
                        pe.wait_ge(s_xlo, k + 1)
                        for wt, acts in ((w_hi, (XH, XL)), (w_lo, (XH,))):
                            for a in acts:
                                for half in range(2):
                                    mm = nc.tensor.matmul(PS[:, half, :], wt[:, 0, k, :], a[:, k, half * HB:(half + 1) * HB],
                                                          start=(k == 0 and wt is w_hi and a is XH),
                                                          stop=(k == 7 and wt is w_lo))
                else:
                    mm = product(pair(n % 2), n, XH, XL)
                mm.then_inc(s_slab, 1)
            take(4)
            for t in range(RNN_T):
                pe.wait_ge(s_clo, t + 1)
                if t:
                    pe.wait_ge(s_sig, 2 * t)
                for g in range(2):
                    for wt, acts in ((w_hi, (XCH, XCL)), (w_lo, (XCH,))):
                        for a in acts:
                            for half in range(2):
                                mm = nc.tensor.matmul(PS[:, 4 + 2 * g + half, :], wt[:, 0, 4 * g + t, :],
                                                      a[:, t, half * HB:(half + 1) * HB],
                                                      start=(wt is w_hi and a is XCH), stop=(wt is w_lo))
                    if t < 3 or g == 0:
                        mm.then_inc(s_gmm, 1)
            mm.then_inc(s_slab, 1)
            for n in range(N_GATE, N_HEADS):
                take(n)
                product(pair(n % 2), n, XH, XL).then_inc(s_slab, 1)

            for j in range(3):
                pe.wait_ge(s_sq, j + 1)
                for half in range(2):
                    mm = nc.tensor.matmul(PS[:, (6 if j == 2 else 4) + half, :], CN[:, C_ONES, :],
                                          SQ[:, 0, half * HB:(half + 1) * HB], start=(j != 1), stop=(j != 0))
                mm.then_inc(s_ss, 1)
            pe.wait_ge(s_llo, 3)
            pe.wait_ge(s_kr, 2)
            UNITS = [(hf, j) for hf in range(2) for j in range(4 * (hf + 1))]

            def project(i, u, part):
                n = N_HEADS + u
                if part == 0:
                    pe.wait_ge(s_w_ready, 2 * i + (n + 1))
                    product(pair(0), n, CQH, CQL, range(2)).then_inc(s_hp, 1)
                elif part == 1:
                    product(pair(1), n, CKH[:, :].unsqueeze(1), CKL[:, :].unsqueeze(1), [2], 2).then_inc(s_hp, 1)
                else:
                    pe.wait_ge(s_qkv, 8 * i + (4 * u + 3))
                    pe.wait_ge(s_rope, 6 * i + (3 * u + 2))
                    for t in range(KT):
                        mm = nc.tensor.matmul(PS[:, 0, 64 * t:64 * t + 64], VR[64:128, t * P:(t + 1) * P], CN[64:128, C_ID, 64:128],
                                              start=True, stop=True)
                    mm.then_inc(s_slab, 1)

            def score_rows(i, u, j):
                b_, kend = 2 * (j % 2), (j + 1) * P
                if j == 0:
                    pe.wait_ge(s_qkv, 8 * i + (4 * u + 4))
                    pe.wait_ge(s_rope, 6 * i + (3 * u + 3))
                if j >= 2:
                    pe.wait_ge(s_mx, 16 * i + (8 * u + j - 1))
                for lo, hi in ((0, min(kend - P, HB)), (HB, kend - P), (kend - P, kend)):
                    if lo < hi:
                        nc.tensor.matmul(PS[:, b_ + lo // HB, lo % HB:lo % HB + hi - lo], Q_[0:96, u % 2, j * P:(j + 1) * P],
                                         K_[0:96, u % 2, lo:hi], start=True, stop=(hi < kend))
                nc.tensor.matmul(PS[:, b_ + j // 4, (j % 4) * P:(j % 4 + 1) * P], ident_b[:, :], negq_b[:, :],
                                 start=False, stop=True).then_inc(s_s, 1)

            def max_row(i, u):
                pe.wait_ge(s_mx, 16 * i + (8 * u + 8))
                for j in range(KT):
                    mm = nc.tensor.matmul(PS[0:1, j // 4, (j % 4) * P:(j % 4 + 1) * P], MX[:, u % 2, j:j + 1], CN[:, C_ID, :],
                                          start=True, stop=True)
                mm.then_inc(s_row, 1)

            def values(i, u, k):
                hf, j = UNITS[k]
                q0 = max(0, j * P - hf * HB)
                if j == 0:
                    pe.wait_ge(s_y, 10 * i + (5 * u + (2 if hf == 0 else 5)))
                pe.wait_ge(s_e, 24 * i + (12 * u + k + 1))
                nc.tensor.matmul(PS[:, 4 + hf, q0:HB], V_[:, u, j, :], PT[:, k % 3, q0:HB],
                                 start=(j == 0), stop=(j == 4 * hf + 3)).then_inc(s_pv, 1)

            def attend(i, u, following):
                pe.wait_ge(s_neg, 2 * i + (u + 1))
                for k, (hf, j) in enumerate(UNITS):
                    q0 = max(0, j * P - hf * HB)
                    if k >= 2:
                        pe.wait_ge(s_e, 24 * i + (12 * u + k - 1))
                    diag = j >= 4 * hf
                    for lo, hi in ((q0, q0 + P), (q0 + P, HB)) if diag else ((q0, HB),):
                        if lo < hi:
                            mm = nc.tensor.matmul(PS[:, 6 + k % 2, lo:hi], K_[0:97, u, j * P:(j + 1) * P],
                                                  Q_[0:97, u, hf * HB + lo:hf * HB + hi], start=True, stop=not (diag and lo == q0))
                            if diag and lo == q0:
                                mm = nc.tensor.matmul(PS[:, 6 + k % 2, lo:hi], ident_b[:, :], negk_b[:, :], start=False, stop=True)
                    mm.then_inc(s_st, 1)
                    if following:
                        if k in (0, 1, 3):
                            project(i, u + 1, min(k, 2))
                        for j2 in MAX_STEPS.get(k, ()):
                            score_rows(i, u + 1, j2)
                        if k == 11:
                            max_row(i, u + 1)
                    if k:
                        values(i, u, k - 1)
                values(i, u, len(UNITS) - 1)

            for part in range(3):
                project(0, 0, part)
            for j in range(KT):
                score_rows(0, 0, j)
            max_row(0, 0)
            with pe.Fori(0, MLA_H // 2 - 1) as i:
                for u in range(2):
                    attend(i, u, True)
            attend(MLA_H // 2 - 1, 0, True)
            attend(MLA_H // 2 - 1, 1, False)
            for n in range(N_OUT_A, N_OUT_A + 8):
                take(n)
                product(pair(n % 2), n, XH, XL, ready=(s_ylo, 0) if n == N_OUT_A else None).then_inc(s_slab, 1)

            def norm_pe(s, total=None):
                if total is not None:
                    s["c"].wait(pe, 7)
                    for half in range(2):
                        mm = nc.tensor.matmul(PS[:, 4 + half, :], CN[:, C_ONES, :], total[:, half * HB:(half + 1) * HB],
                                              start=True, stop=True)
                    mm.then_inc(s["cs"].sem, 1)
                for k in range(KT):
                    s["sq"].wait(pe, k + 1)
                    for half in range(2):
                        mm = nc.tensor.matmul(PS[:, 6 + half, :], CN[:, C_ONES, :], SQN[:, k % 2, half * HB:(half + 1) * HB],
                                              start=(k == 0), stop=(k == KT - 1))
                    mm.then_inc(s["ss"].sem, 1)

            norm_pe(ln1, MU[:, :])

            take(N_DT)
            product(pair(N_DT % 2), N_DT, XH, XL, ready=(ln1["lo"].sem, ln1["lo"].base)).then_inc(s_slab, 1)
            pe.wait_ge(s_evac[N_DT % 2], N_DT // 2 + 1)
            for c in range(CHUNKS):
                mm = nc.tensor.matmul(PS[:, 7, SSD_HEADS * c:SSD_HEADS * (c + 1)], DTR[0:SSD_HEADS, c * P:(c + 1) * P],
                                      CN[0:SSD_HEADS, C_ID, 0:SSD_HEADS], start=True, stop=True)
            mm.then_inc(s_dtt, 1)
            def spread(n, g, same_pair):
                pe.wait_ge(s_w_ready, SSD_SLABS * g + (n + 1))
                m = n - 1 if same_pair else n - 2
                pe.wait_ge(s_evac[m % 2], (SSD_SLABS // 2) * g + m // 2 + 1)

            def into_pair(n, g):
                spread(n, g, False)
                product(pair(n % 2), n, XH, XL).then_inc(s_slab, 1)

            def z_tiles(g, step, place):
                n, third = N_CORE + step // 3, step % 3
                tiles = range(3 * third, 3 * third + 1) if place == 1 else range(3 * third + 1, min(3 * third + 3, 8))
                if tiles[0] == 0:
                    spread(n, g, True)
                mm = product(pair(0), n, XH, XL, tiles, 0, range(8))
                if tiles[-1] == 7:
                    mm.then_inc(s_slab, 1)

            def core(g):
                pe.wait_ge(s_cs, 6 * g + 6)
                for step in range(CHUNKS + 2):
                    c = step
                    if c < CHUNKS:
                        tok = slice(c * P, (c + 1) * P)
                        if c:
                            pe.wait_ge(s_a, 24 * g + 3 * c)
                            pe.wait_ge(s_bk, 8 * g + c)
                        if c >= 2:
                            pe.wait_ge(s_b, 32 * g + (4 * c - 6))
                        nc.tensor.matmul(PS[:, 4, 0:P], BT[:, tok], CT[:, tok], start=True, stop=True)
                        nc.tensor.transpose(PS[:, 4, P:2 * P], BT[:, tok], CN[:, C_ID, :])
                        if c >= 3:
                            pe.wait_ge(s_c, 32 * g + 4 * (c - 2))
                        for m in range(4):
                            mm = nc.tensor.transpose(PS[:, 5, m * P:(m + 1) * P], XS[:, m, tok], CN[:, C_ID, :])
                        mm.then_inc(s_cb, 1)
                        pe.wait_ge(s_av, 8 * g + (c + 1))
                        if c:
                            pe.wait_ge(s_ex, 8 * g + c)
                        for b in range(2):
                            mm = nc.tensor.matmul(PS[:, 6 + b, :], CN[:, C_AFTER, :],
                                                  AV[:, 4 * b:4 * b + 4, :].rearrange("p h l -> p (h l)"), start=True, stop=True)
                        mm.then_inc(s_seg, 1)
                    if step < 9:
                        z_tiles(g, step, 1)
                    c = step - 1
                    if 0 <= c < CHUNKS:
                        tok = slice(c * P, (c + 1) * P)
                        pe.wait_ge(s_m, 8 * g + (c + 1))
                        if c:
                            pe.wait_ge(s_b, 32 * g + 4 * c)
                        for h in range(HPG):
                            nc.tensor.matmul(PS[:, 2, 64 * h:64 * h + 64], E[:, c % 2, h, :], XF[:, c % 2, 64 * h:64 * h + 64],
                                             start=True, stop=True)
                        nc.tensor.matmul(PS[:, 3, :], CT[:, tok], ST[:, :], start=True, stop=True)
                        after = min(c + 2, CHUNKS)
                        pe.wait_ge(s_bk, 8 * g + after)
                        pe.wait_ge(s_a, 24 * g + 3 * after)
                        nc.tensor.matmul(PS[:, 4, :], BK[:, c % 2, :], XFD[:, c % 2, :], start=True, stop=True).then_inc(s_core, 1)
                    c = step - 2
                    if 0 <= c < CHUNKS:
                        pe.wait_ge(s_b, 32 * g + (4 * c + 4))
                        if c:
                            pe.wait_ge(s_c, 32 * g + 4 * c)
                        for m in range(4):
                            mm = nc.tensor.transpose(PS[:, 5, m * P:(m + 1) * P], YR[:, 1, m * P:(m + 1) * P], CN[:, C_ID, :])
                        mm.then_inc(s_yt, 1)
                    if step < 9:
                        z_tiles(g, step, 2)

            def square_sums(g):
                for m in range(4):
                    pe.wait_ge(s_gs, 4 * g + (m + 1))
                    sq = AV[:, :, :] if m % 2 == 0 else E[:, 1, :, :]
                    for half in range(2):
                        mm = nc.tensor.matmul(PS[:, 4 + half, :], CN[:, C_ONES, :],
                                              sq[:, 4 * half:4 * half + 4, :].rearrange("p h l -> p (h l)"),
                                              start=(m == 0), stop=(m == 3))
                    mm.then_inc(s_gss, 1)

            def out_slabs(n0, g):
                for q in range(4):
                    n = n0 + q
                    pe.wait_ge(s_w_ready, SSD_SLABS * g + (n + 1))
                    for e in range(2):
                        if q:
                            if e == 0:
                                pe.wait_ge(s_oe, 4 * g + q)
                            else:
                                pe.wait_ge(s_evac[(n - 1) % 2], (SSD_SLABS // 2) * g + (n - 1) // 2 + 1)
                        mm = product(pair(2 + e), n, YH, YL, range(4 * e, 4 * e + 4), 4 * e,
                                     ready=(s_gl, 4 * g) if q == 0 and e == 0 else None)
                        if e == 0:
                            mm.then_inc(s_oh, 1)
                    mm.then_inc(s_slab, 1)

            for n in range(N_SSD, N_CORE):
                take(n)
                product(pair(n % 2), n, XH, XL).then_inc(s_slab, 1)
                if n == N_SSD + 1:
                    pe.wait_ge(s_dt, DT_STEPS)
                    for b, cst in ((4, C_AFTER), (5, C_UPTO), (6, C_ONES)):
                        mm = nc.tensor.matmul(PS[:, b, 0:256], CN[:, cst, :], DTS[:, 1, :], start=True, stop=True)
                    mm.then_inc(s_dtp, 1)
            pe.wait_ge(s_dta, 5)
            with pe.Fori(0, GROUPS - 1) as g:
                core(g)
                pe.wait_ge(s_evac[(N_CORE + 2) % 2], (SSD_SLABS // 2) * g + (N_CORE + 2) // 2 + 1)
                into_pair(N_CORE + 3, g)
                square_sums(g)
                into_pair(N_CORE + 4, g)
                out_slabs(N_CORE + 5, g)
                for n in range(N_CORE + 9, N_CORE + 14):
                    into_pair(n, g)
            core(GROUPS - 1)
            square_sums(GROUPS - 1)
            out_slabs(N_CORE + 3, GROUPS - 1)
            norm_pe(ln2, SUM2)
            norm_pe(mix)
            def stream(n0, count, hi, lo, ready=None):
                for n in (n0, n0 + 1):
                    take(n)
                    product(pair(n % 2), n, hi, lo, ready=ready if n == n0 else None).then_inc(s_slab, 1)
                with pe.Fori(1, count // 2) as i:
                    for e in range(2):
                        n = n0 + e
                        pe.wait_ge(s_w_ready, 2 * i + (n + 1))
                        pe.wait_ge(s_evac[n % 2], i + n // 2)
                        product(pair(n % 2), n, hi, lo).then_inc(s_slab, 1)

            stream(N_IN2, 12, XH, XL, (mix["lo"].sem, mix["lo"].base))
            with pe.Fori(0, 2) as i:
                for mm_ in range(2):
                    def at(per, k):
                        return (2 * per) * i + (per * mm_ + k)

                    for q in range(3):
                        n = N_SB + 3 * mm_ + q
                        pe.wait_ge(s_w_ready, 6 * i + (n + 1))
                        pe.wait_ge(s_evac[n % 2], 3 * i + n // 2)
                        pe.wait_ge(s_at, at(4, 1))
                        product(pair(n % 2), n, XH, XL).then_inc(s_slab, 1)
                    for q in range(3):
                        n = N_SB + 3 * mm_ + q
                        pe.wait_ge(s_evac[n % 2], 3 * i + n // 2 + 1)
                    for t in range(KT):
                        mm = nc.tensor.transpose(PS[:, 6 + t // 4, (t % 4) * P:(t % 4 + 1) * P], VT[:, t * P:(t + 1) * P], CN[:, C_ID, :])
                    mm.then_inc(s_vt, 1)
                    pe.wait_ge(s_vc, at(1, 1))

                    for step in range(NU + 2):
                        t = step
                        if t < NU:
                            hf, j = SB_UNITS[t]
                            q0 = max(0, j * P - hf * HB)
                            if t >= 2:
                                pe.wait_ge(s_ls, at(NU, t - 1))
                            for u in range(2):
                                o = slice(64 * u, 64 * u + 64)
                                mm = nc.tensor.matmul(pair(3 * (t % 2))[:, u, q0:HB], KH[o, j * P:(j + 1) * P],
                                                      QH[o, hf * HB + q0:(hf + 1) * HB], start=True, stop=True)
                            mm.then_inc(s_z, 1)
                        t = step - 2
                        if t >= 0:
                            hf, j = SB_UNITS[t]
                            q0, first, end = max(0, j * P - hf * HB), j == 4 * hf + 3, j == 0
                            pe.wait_ge(s_d, at(NU, t + 1))
                            if not end:
                                for u in range(2):
                                    nc.tensor.matmul(PS[:, 2 + u, q0:HB], CN[:, C_UPTO, :], SB_P[:, t % 3, u, q0:HB],
                                                     start=False, stop=True, skip_group_check=True)
                            pe.wait_ge(s_w, at(NU, t + 1))
                            if first and hf == 1:
                                pe.wait_ge(s_at, at(4, 3))
                            for u in range(2):
                                mm = nc.tensor.matmul(PS[0:64, 4 + u, q0:HB], VH[:, j, 64 * u:64 * u + 64], SB_A[:, t % 3, u, q0:HB],
                                                      start=first, stop=True, skip_group_check=True)
                            mm.then_inc(s_o, 1)
                        t = step - 1
                        if 0 <= t < NU:
                            hf, j = SB_UNITS[t]
                            q0, first = max(0, j * P - hf * HB), j == 4 * hf + 3
                            pe.wait_ge(s_sp, at(NU, t + 1))
                            if first and hf == 1:
                                pe.wait_ge(s_d, at(NU, 4))
                            for u in range(2):
                                mm = nc.tensor.matmul(PS[:, 2 + u, q0:HB], CN[:, C_AFTER, :], SB_P[:, t % 3, u, q0:HB],
                                                      start=first, stop=True, skip_group_check=True)
                            mm.then_inc(s_su, 1)
            for k in range(8):
                pe.wait_ge(s_hq, k + 1)
                if k >= 2:
                    pe.wait_ge(s_hv, k - 1)
                for half in range(2):
                    mm = nc.tensor.matmul(PS[:, 4 + 2 * (k % 2) + half, :], CN[:, C_BLK, :], HQ[:, k % 2, half * HB:(half + 1) * HB],
                                          start=True, stop=True)
                mm.then_inc(s_hs, 1)
            stream(N_OUT2, 8, XH, XL, (s_hl, 0))
            norm_pe(mlp)

            def up(b, n0, dyn, first=False):
                for q in range(4):
                    n = n0 + q
                    pe.wait_ge(s_w_ready, 2 * dyn + (n + 1) if dyn is not None else n + 1)
                    pe.wait_ge(s_evac[n % 2], dyn + n // 2 if dyn is not None else n // 2)
                    product(pair(n % 2), n, XH, XL,
                            ready=(mlp["lo"].sem, mlp["lo"].base) if dyn is None and q == 0 else None).then_inc(s_slab, 1)

            def down(b, n0, turn, done):
                for q in range(4):
                    n = n0 + q
                    dyn = 0 if turn is None else 8 * turn
                    pe.wait_ge(s_w_ready, 2 * dyn + (n + 1))
                    if q == 0:
                        pe.wait_ge(s_fl, 4 * done + 4)
                    pe.wait_ge(s_fe, 4 * done + q + 1)
                    pe.wait_ge(s_evac[(n - 1) % 2], dyn + (n - 1) // 2 + 1)
                    for e in range(2):
                        mm = product(pair(2 + e), n, UH[:, b % 2, :, :], UL[:, b % 2, :, :], range(4 * e, 4 * e + 4), 4 * e)
                        if e == 0:
                            mm.then_inc(s_fo, 1)
                    mm.then_inc(s_slab, 1)

            up(0, N_FFN, None)
            with pe.Fori(0, 3) as i:
                for e in range(2):
                    up(1 + e, N_FFN + 4 + 8 * e, 8 * i)
                    down(e, N_FFN + 8 + 8 * e, i, 2 * i + e)
            up(7, N_FFN + 52, None)
            down(6, N_FFN + 56, None, 6)
            down(7, N_FFN + 60, None, 7)
            pe.wait_ge(s_pw, 2)
            for q in range(2):
                n = N_PLE + q
                pe.wait_ge(s_w_ready, n + 1)
                for m in range(4):
                    g = 4 * q + m
                    if g >= 2:
                        pe.wait_ge(s_pj, g - 1)
                    mm = product(pair(g % 2), n, PH, PL, range(2 * m, 2 * m + 2), 2 * m)
                    mm.then_inc(s_pm if m < 3 else s_slab, 1)
            norm_pe(ple)
            pe.wait_ge(s_pj, 8)
            pe.wait_ge(s_evac[0], (N_PLE + 1) // 2 + 1)
            stream(N_PLE + 2, 8, XH, XL, (ple["lo"].sem, ple["lo"].base))
            norm_pe(fin)

        @block.scalar
        def _(act):
            def inverse_root(dst, src, width, eps, sem, count, done):
                nc.scalar.activation(dst, src, ACT.Ln, scale=1.0 / width, bias=eps).then_inc(sem, 1)
                act.wait_ge(sem, count + 1)
                nc.scalar.activation(dst, dst, ACT.Exp, scale=-0.5).then_inc(done, 1)

            for j in range(4):
                act.dma_start(H[:, 2 * j:2 * j + 2, :], x_t[2 * j:2 * j + 2, :, :].rearrange("k p t -> p k t")).then_inc(s_x[j], 16)
                if j == 0:
                    act.dma_start(VC[:, :], vec).then_inc(s_const, 16)
                    act.dma_start(CN[:, :, :], consts).then_inc(s_const, 16)
                    act.dma_start(RW[:, :], rows).then_inc(s_const, 16)
            for k in range(8):
                if k % 2 == 0:
                    act.wait_ge(s_x[k // 2], 16)
                nc.scalar.activation(XH[:, k, :], H[:, k, :], ACT.Copy).then_inc(s_xhi, 1)
            act.wait_ge(s_const, 48)
            nc.scalar.activation(SM[:, 0, 0:4], col("lam", 0, 4), ACT.Abs).then_inc(s_lama, 1)
            act.wait_ge(s_lama, 1)
            nc.scalar.activation(SM[:, 1, 0:4], SM[:, 0, 0:4], ACT.Exp, scale=-1.0).then_inc(s_lama, 1)
            for t in range(RNN_T):
                act.wait_ge(s_evac[t % 2], t // 2 + 1)
                nc.scalar.activation(XCH[:, t, :], H[:, 4 + t, :], ACT.Copy).then_inc(s_chi, 1)
            for t in range(RNN_T):
                act.wait_ge(s_gmm, min(2 * t + 1, 7))
                nc.scalar.activation(R[:, t, :], flat(2), ACT.Sigmoid, bias=col("ba", t)).then_inc(s_sig, 1)
                if t < 3:
                    act.wait_ge(s_gmm, 2 * t + 2)
                    nc.scalar.activation(I_[:, t, :], flat(3), ACT.Sigmoid, bias=col("bx", t)).then_inc(s_sig, 1)
                else:
                    act.wait_ge(s_slab, N_GATES + 1)
                    nc.scalar.activation(I_[:, t, :], flat(3), ACT.Sigmoid, bias=col("bx", t)).then_inc(s_evac[0], 1)
            act.wait_ge(s_lam, 24)
            for t in range(RNN_T):
                if t:
                    act.wait_ge(s_rd, 5 * t)
                nc.scalar.activation(A_[:, 0, :], R[:, t, :], ACT.Exp, scale=SM[:, 8, t:t + 1]).then_inc(s_ra, 1)
                nc.scalar.activation(R[:, t, :], R[:, t, :], ACT.Tanh, scale=SM[:, 9, t:t + 1]).then_inc(s_ra, 1)
                n = N_GATE + t
                act.wait_ge(s_slab, n + 1)
                nc.scalar.activation(H[:, t, :], flat(n % 2), ACT.Silu).then_inc(s_evac[n % 2], 1)
                act.wait_ge(s_rd, 5 * t + 2)
                nc.scalar.activation(T_[:, 0, :], T_[:, 0, :], ACT.Sqrt).then_inc(s_ra, 1)
            for t in range(RNN_T):
                n = N_GATE + 4 + t
                act.wait_ge(s_slab, n + 1)
                act.wait_ge(s_yr, t + 1)
                nc.scalar.activation(H[:, 4 + t, :], flat(n % 2), ACT.Silu).then_inc(s_evac[n % 2], 1)
            act.dma_start(Q_[64:128, 0, :].bitcast(I32), pos.partition_broadcast(64)).then_inc(s_pos, 16)
            for j in range(3):
                n = N_LAT + j
                if j == 0:
                    act.wait_ge(s_tr, 12)
                    nc.scalar.activation(TRIG[64:128, :], AN[64:128, 0, :], ACT.Sin).then_inc(s_sin, 1)
                    act.wait_ge(s_sin, 1)
                act.wait_ge(s_slab, n + 1)
                nc.scalar.activation(CQ[:, j, :], flat(n % 2), ACT.Copy).then_inc(s_evac[n % 2], 1)
                act.wait_ge(s_evac[n % 2], n // 2 + 1)
                if j:
                    act.wait_ge(s_ss, j)
                nc.scalar.activation(SQ[:, 0, :], CQ[:, j, :], ACT.Square).then_inc(s_sq, 1)
            for r in range(2):
                if r == 0:
                    nc.scalar.preload_act_table_set("natural_log_exp_and_others")
                act.wait_ge(s_ss, r + 2)
                inverse_root(Q_[:, r, :], flat(2 + r), 256 >> r, EPS6, s_rs, 2 * r, s_rs)
            for j in range(3):
                act.wait_ge(s_lat, j + 1)
                nc.scalar.activation(CQH[:, j, :] if j < 2 else CKH[:, :], CQ[:, j, :], ACT.Copy).then_inc(s_lhi, 1)
            act.wait_ge(s_llo, 3)
            def head_copy(i, u, part):
                if part < 2:
                    act.wait_ge(s_hp, 4 * i + (2 * u + part + 1))
                    dst = Q_ if part == 0 else K_
                    nc.scalar.activation(dst[0:64, u % 2, :], flat(part)[0:64, :], ACT.Copy).then_inc(s_qkv, 1)
                    if part == 1:
                        nc.scalar.activation(VR[64:128, :], flat(1)[64:128, :], ACT.Copy).then_inc(s_qkv, 1)
                else:
                    act.wait_ge(s_slab, 2 * i + (N_HEADS + u + 1))
                    nc.scalar.activation(V_[:, u % 2, :, 0:64], PS[:, 0, :].rearrange("p (t d) -> p t d", d=64), ACT.Copy).then_inc(s_qkv, 1)

            def exponentials(i, u, following):
                units = [(hf, j) for hf in range(2) for j in range(4 * (hf + 1))]
                for k, (hf, j) in enumerate(units):
                    q0 = max(0, j * P - hf * HB)
                    act.wait_ge(s_st, 24 * i + (12 * u + k + 1))
                    if k >= 3:
                        act.wait_ge(s_pv, 24 * i + (12 * u + k - 2))
                    nc.scalar.activation(PT[:, k % 3, q0:HB], PS[:, 6 + k % 2, q0:HB], ACT.Exp, scale=MLA_SCALE).then_inc(s_e, 1)
                    if following and k in (0, 1, 3):
                        head_copy(i, u + 1, min(k, 2))

            for part in range(3):
                head_copy(0, 0, part)
            with act.Fori(0, MLA_H // 2 - 1) as i:
                for u in range(2):
                    exponentials(i, u, True)
            exponentials(MLA_H // 2 - 1, 0, True)
            exponentials(MLA_H // 2 - 1, 1, False)
            act.wait_ge(s_slab, N_OUT_A)
            act.wait_ge(s_evac[(N_OUT_A - 1) % 2], (N_OUT_A - 1) // 2 + 1)

            def x_again(k):
                act.dma_start(XR[:, k % 2, :], x_t[k, :, :]).then_inc(s_xr[k % 2], 16)

            x_again(0)
            x_again(1)
            for k in range(KT):
                nc.scalar.activation(XH[:, k, :], H[:, k, :], ACT.Copy).then_inc(s_yhi, 1)
            for k in range(2, KT):
                n = N_OUT_A + k - 2
                act.wait_ge(s_evac[n % 2], n // 2 + 1)
                x_again(k)

            def norm_act(s, bias=None, split=True, ready=None):
                eps = EPS5 if bias else EPS6
                for k in range(KT):
                    if bias:
                        s["c"].wait(act, k + 9)
                    elif isinstance(ready, Tiles):
                        ready.wait(act, k)
                    elif isinstance(ready, Part):
                        ready.wait(act, k + 1)
                    else:
                        act.wait_ge(ready, k + 1)
                    if k >= 2:
                        s["ss"].wait(act, k - 1)
                    nc.scalar.activation(SQN[:, k % 2, :], H[:, k, :], ACT.Square).then_inc(s["sq"].sem, 1)
                nc.scalar.preload_act_table_set("natural_log_exp_and_others")
                s["ss"].wait(act, KT)
                inverse_root(RS[:, :], flat(3), D, eps, s["v"].sem, s["v"].base, s["rs"].sem)
                for k in range(KT):
                    s["t"].wait(act, k + 1)
                    src = TN[:, k % 2, :]
                    if not bias and not split:
                        act.dma_start(out[k, :, :], src).then_inc(s_st_out[k % 2], 16)
                        if k == KT - 1:
                            for e in range(2):
                                act.wait_ge(s_st_out[e], 16 * KT // 2)
                        continue
                    if bias:
                        nc.scalar.activation(H[:, k, :], src, ACT.Identity, bias=col(bias, k)).then_inc(s["h"].sem, 1)
                        s["h"].wait(act, k + 1)
                        src = H[:, k, :]
                    if split:
                        nc.scalar.activation(XH[:, k, :], src, ACT.Copy).then_inc(s["hi"].sem, 1)

            norm_act(ln1, "ln1_b")
            act.wait_ge(s_slab, N_DT + 1)
            nc.scalar.activation(DTR[0:SSD_HEADS, :], flat(N_DT % 2)[0:SSD_HEADS, :], ACT.Copy).then_inc(s_evac[N_DT % 2], 1)
            act.wait_ge(s_dt, 1)
            e_, ab_ = AV[:, 0:2, :].rearrange("p a b -> p (a b)"), AV[:, 2:4, :].rearrange("p a b -> p (a b)")
            nc.scalar.activation(ab_, DTS[:, 0, :], ACT.Abs).then_inc(s_dta, 1)
            act.wait_ge(s_dta, 1)
            nc.scalar.activation(e_, ab_, ACT.Exp, scale=-1.0).then_inc(s_dta, 1)
            nc.scalar.activation(RW[:, 64:96], RW[:, 32:64], ACT.Exp).then_inc(s_dta, 1)
            act.wait_ge(s_dtp, 1)
            nc.scalar.activation(DTS[:, 2, :], PS[:, 4, 0:256], ACT.Exp).then_inc(s_dta, 1)
            nc.scalar.activation(DTS[:, 3:5, :], PS[:, 5:7, 0:256], ACT.Exp).then_inc(s_dta, 1)
            def silu_conv(n, q, g):
                act.wait_ge(s_evac[n % 2], (SSD_SLABS // 2) * g + n // 2 + 1)
                dst = BT[:, :] if q == 0 else CT[:, :] if q == 1 else XS[:, q - 2, :]
                nc.scalar.activation(dst, CV[:, q % 2, :], ACT.Silu).then_inc(s_cs, 1)

            def silu_z(n, m, b, g):
                act.wait_ge(s_slab, SSD_SLABS * g + (n + 1))
                nc.scalar.activation(Z[:, m, :], flat(b), ACT.Silu).then_inc(s_evac[n % 2], 1)

            def raw_z(m, g):
                n = N_CORE - 1 + m
                act.wait_ge(s_slab, SSD_SLABS * g + (n + 1))
                nc.scalar.activation(Z[:, m, :], flat(0), ACT.Copy).then_inc(s_evac[n % 2], 1)

            def core(g):
                for c in range(CHUNKS):
                    act.wait_ge(s_cb, 8 * g + (c + 1))
                    nc.scalar.activation(BK[:, c % 2, :], PS[:, 4, P:2 * P], ACT.Copy).then_inc(s_bk, 1)
                    act.wait_ge(s_seg, 8 * g + (c + 1))
                    if c >= 2:
                        act.wait_ge(s_core, 8 * g + (c - 1))
                    nc.scalar.activation(E[:, c % 2, :, :].rearrange("p (b h) l -> p b (h l)", b=2), PS[:, 6:8, :], ACT.Exp).then_inc(s_ex, 1)
                    if c in (3, 6):
                        raw_z(c // 3, g)
                raw_z(3, g)
                for m in range(1, 4):
                    n = N_CORE - 1 + m
                    act.wait_ge(s_evac[n % 2], (SSD_SLABS // 2) * g + n // 2 + 1)
                    nc.scalar.activation(Z[:, m, :], Z[:, m, :], ACT.Silu).then_inc(s_zs, 1)

            def square(m, g):
                act.wait_ge(s_g, 4 * g + (m + 1))
                if m >= 2:
                    act.wait_ge(s_gss, 4 * g + (m - 1))
                sq = AV[:, :, :] if m % 2 == 0 else E[:, 1, :, :]
                nc.scalar.activation(sq.rearrange("p h l -> p (h l)"), XS[:, m, :], ACT.Square).then_inc(s_gs, 1)

            def after(g):
                for m in range(4):
                    square(m, g)
                nc.scalar.preload_act_table_set("natural_log_exp_and_others")
                act.wait_ge(s_gss, 4 * g + 4)
                inverse_root(E[:, 0, :, :].rearrange("p h l -> p (h l)"), flat(2), 512, EPS6, s_gv, g, s_gr)
                for m in range(4):
                    act.wait_ge(s_gt, 4 * g + (m + 1))
                    nc.scalar.activation(YH[:, m, :], CV[:, m % 2, :], ACT.Copy).then_inc(s_gh, 1)

            for q in range(6):
                silu_conv(N_SSD + q, q, 0)
            silu_z(N_SSD + 6, 0, 0, 0)
            with act.Fori(0, GROUPS - 1) as g:
                core(g)
                after(g)
                for q in range(6):
                    silu_conv(N_CORE + (3 + q if q < 2 else 7 + q), q, g)
                silu_z(N_CORE + 13, 0, 0, g)
            core(GROUPS - 1)
            after(GROUPS - 1)
            ln2["c"].wait(act, 8)
            norm_act(ln2, "ln2_b", False)
            norm_act(mix, None, True, ln2["h"])
            def copy_slab(n, dst, dyn=0, half=0, scale=1.0):
                act.wait_ge(s_slab, dyn + (n + 1))
                nc.scalar.activation(dst, flat(n % 2), ACT.Copy, scale=scale).then_inc(s_evac[n % 2], 1)

            for m in range(4):
                if m:
                    act.wait_ge(s_cc, 4 * m - 3)
                copy_slab(N_IN2 + 3 * m, CC)
            with act.Fori(0, 2) as i:
                for mm_ in range(2):
                    def at(per, k):
                        return (2 * per) * i + (per * mm_ + k)

                    for q, dst in enumerate((QH, KH, VT)):
                        copy_slab(N_SB + 3 * mm_ + q, dst[:, :], 6 * i, 3 * i, SB_SCALE if q == 0 else 1.0)
                    act.wait_ge(s_vt, at(1, 1))
                    nc.scalar.activation(VH[:, :, :].rearrange("p t d -> p (t d)"), flat(3), ACT.Copy).then_inc(s_vc, 1)
                    nc.scalar.preload_act_table_set("natural_log_exp_and_others")
                    for step in range(NU + 1):
                        t = step
                        if t < NU:
                            hf, j = SB_UNITS[t]
                            q0 = max(0, j * P - hf * HB)
                            z, l = pair(3 * (t % 2))[:, :, q0:HB], SB_L[:, t % 2, :, q0:HB]
                            act.wait_ge(s_z, at(NU, t + 1))
                            if t >= 2:
                                act.wait_ge(s_sp, at(NU, t - 1))
                            nc.scalar.activation(l, z, ACT.Abs).then_inc(s_al, 1)
                            act.wait_ge(s_al, at(3 * NU, 3 * t + 1))
                            nc.scalar.activation(l, l, ACT.Exp, scale=-1.0).then_inc(s_al, 1)
                            act.wait_ge(s_al, at(3 * NU, 3 * t + 2))
                            nc.scalar.activation(l, l, ACT.Ln, bias=1.0).then_inc(s_al, 1)
                        t = step - 1
                        if t >= 0:
                            hf, j = SB_UNITS[t]
                            q0 = max(0, j * P - hf * HB)
                            act.wait_ge(s_d, at(NU, t + 1))
                            nc.scalar.activation(SB_A[:, t % 3, :, q0:HB], SB_A[:, t % 3, :, q0:HB], ACT.Exp).then_inc(s_w, 1)
            act.wait_ge(s_at, 17)
            for k in range(9):
                if k < 8:
                    src = CONV[:, k, :] if k < 4 else ATT[:, k - 4, :]
                    if k >= 2:
                        act.wait_ge(s_hs, k - 1)
                    nc.scalar.activation(HQ[:, k % 2, :], src, ACT.Square).then_inc(s_hq, 1)
                if k:
                    if k == 1:
                        nc.scalar.preload_act_table_set("natural_log_exp_and_others")
                    act.wait_ge(s_hs, k)
                    if k >= 3:
                        act.wait_ge(s_ht, k - 2)
                    inverse_root(HR[:, (k - 1) % 2, :], flat(2 + (k - 1) % 2), 64, EPS6, s_hv, k - 1, s_hr)
                    act.wait_ge(s_ht, k)
                    nc.scalar.activation(XH[:, k - 1, :], HT[:, (k - 1) % 2, :], ACT.Copy).then_inc(s_hh, 1)

            norm_act(mlp, None, True, Tiles(N_OUT2))

            def relu(n, parity, dyn, count, hi):
                act.wait_ge(s_slab, dyn + (n + 1))
                nc.scalar.activation(FT[:, parity, :], flat(n % 2), ACT.Relu).then_inc(s_evac[n % 2], 1)
                act.wait_ge(s_ff, count + 1)
                nc.scalar.activation(hi, FT[:, parity, :], ACT.Copy).then_inc(s_fh, 1)

            def up(b, n0, turn):
                dyn, cnt = (0, 4 * b) if turn is None else (16 * turn, 8 * turn + 4 * b)
                for q in range(4):
                    if q >= 2 or b:
                        act.wait_ge(s_fl, cnt + (q - 1))
                    relu(n0 + q, q % 2, dyn, cnt + q, UH[:, b % 2, q, :])

            up(0, N_FFN, None)
            with act.Fori(0, 3) as i:
                for e in range(2):
                    if e == 1:
                        act.wait_ge(s_slab, 16 * i + (N_FFN + 12))
                    else:
                        act.wait_ge(s_slab, 16 * i + (N_FFN + 4))
                    up(1 + e, N_FFN + 4 + 8 * e, i)
            up(7, N_FFN + 52, None)
            act.wait_ge(s_fl, 32)
            act.dma_start(XR[:, :, :], p_t.rearrange("k p t -> p k t")).then_inc(s_pl, 16)
            act.wait_ge(s_pl, 16)
            act.wait_ge(s_slab, N_PLE)
            for k in range(2):
                nc.scalar.activation(PH[:, k, :], XR[:, k, :], ACT.Copy).then_inc(s_ph, 1)
            for g in range(8):
                q, m = divmod(g, 4)
                if m < 3:
                    act.wait_ge(s_pm, 3 * q + m + 1)
                else:
                    act.wait_ge(s_slab, N_PLE + q + 1)
                nc.scalar.activation(PJ[:, g, :], flat(g % 2), ACT.Copy).then_inc(s_pj, 1)
            act.wait_ge(s_pj, 8)
            for q in range(2):
                nc.scalar.activation(SM[:, q, 0:1], SM[:, 2, 0:1], ACT.Copy).then_inc(s_evac[(N_PLE + q) % 2], 1)
            act.wait_ge(s_fe, 33)
            norm_act(ple, None, True, Done())
            for k in range(KT):
                n = N_PLE + 2 + k
                act.wait_ge(s_slab, n + 1)
                if k >= 2:
                    act.wait_ge(s_h3, k - 1)
                nc.scalar.activation(XR[:, k % 2, :], flat(n % 2), ACT.Sigmoid).then_inc(s_evac[n % 2], 1)
            norm_act(fin, None, False, s_h3)

        @block.vector
        def _(dve):
            v = nc.vector
            setup = Tally(dve, s_setup)
            conv = Tally(dve, s_conv)
            for k in range(8):
                dve.wait_ge(s_xhi, k + 1)
                v.tensor_tensor(XL[:, k, :], H[:, k, :], XH_f[:, k, :], ALU.subtract).then_inc(s_xlo, 1)
                if k == 0:
                    dve.wait_ge(s_const, 48)
                    for a, b in ((ident_b, C_ID), (negq_b, C_NEGQ), (negk_b, C_NEGK)):
                        setup(v.tensor_copy(a[:, :], CN[:, b, :]))

            def log1p_steps(out, e, s, s2, t, tally):
                tally(v.tensor_scalar(t, e, 2.0, None, ALU.add)); tally.wait()
                tally(v.reciprocal(t, t)); tally.wait()
                tally(v.tensor_tensor(s, e, t, ALU.mult)); tally.wait()
                tally(v.tensor_tensor(s2, s, s, ALU.mult)); tally.wait()
                tally(v.tensor_scalar(t, s2, 2.0 / 15, 2.0 / 13, ALU.mult, ALU.add)); tally.wait()
                for q in (11, 9, 7, 5, 3, 1):
                    tally(v.tensor_tensor(t, t, s2, ALU.mult)); tally.wait()
                    tally(v.tensor_scalar(t, t, 2.0 / q, None, ALU.add)); tally.wait()
                tally(v.tensor_tensor(out, t, s, ALU.mult)); tally.wait()

            lam = Tally(dve, s_lam)
            lam(v.memset(EPS5, 1e-5))
            lam(v.memset(EPS6, 1e-6))
            L = SM[:, :, 0:4]
            dve.wait_ge(s_lama, 2)
            log1p_steps(L[:, 2, :], L[:, 1, :], L[:, 3, :], L[:, 4, :], L[:, 5, :], lam)
            lam(v.tensor_scalar(L[:, 3, :], col("lam", 0, 4), -1.0, 0.0, ALU.mult, ALU.max)); lam.wait()
            lam(v.tensor_tensor(L[:, 2, :], L[:, 2, :], L[:, 3, :], ALU.add)); lam.wait()
            lam(v.tensor_scalar(SM[:, 8, 0:4], L[:, 2, :], -RG_C, None, ALU.mult))
            lam(v.tensor_scalar(SM[:, 9, 0:4], L[:, 2, :], RG_C, None, ALU.mult))
            for t in range(RNN_T):
                dve.wait_ge(s_slab, t + 1)
                src, y = flat(t % 2), H[:, 4 + t, :]
                conv(v.tensor_scalar(y, src, col("conv_w", 12 + t), col("conv_b", t), ALU.mult, ALU.add)); conv.wait()
                for d in (1, 2, 3):
                    ins = v.scalar_tensor_tensor(out=y[:, d:TOK], in0=src[:, 0:TOK - d], scalar=col("conv_w", 4 * (3 - d) + t),
                                                 in1=y[:, d:TOK], op0=ALU.mult, op1=ALU.add)
                    if d < 3:
                        conv(ins)
                        conv.wait()
                    else:
                        ins.then_inc(s_evac[t % 2], 1)
                        dve.wait_ge(s_evac[t % 2], t // 2 + 1)
                dve.wait_ge(s_chi, t + 1)
                v.tensor_tensor(XCL[:, t, :], y, XCH[:, t, :].bitcast(F32), ALU.subtract).then_inc(s_clo, 1)
            ra, rd = s_ra, Tally(dve, s_rd)
            for t in range(RNN_T):
                x_c = H[:, 4 + t, :]
                dve.wait_ge(s_ra, 3 * t + 1)
                rd(v.tensor_tensor(T_[:, 0, :], A_[:, 0, :], A_[:, 0, :], ALU.mult)); rd.wait()
                dve.wait_ge(s_ra, 3 * t + 2)
                rd(v.scalar_tensor_tensor(out=T_[:, 0, :], in0=T_[:, 0, :], scalar=1.0, in1=R[:, t, :],
                                          op0=ALU.add, op1=ALU.mult))
                if t < 3:
                    dve.wait_ge(s_sig, 2 * t + 2)
                else:
                    dve.wait_ge(s_evac[0], 3)
                rd(v.tensor_tensor(I_[:, t, :], I_[:, t, :], x_c, ALU.mult)); rd.wait()
                dve.wait_ge(s_ra, 3 * t + 3)
                rd(v.tensor_tensor(I_[:, t, :], I_[:, t, :], T_[:, 0, :], ALU.mult)); rd.wait()
                rd(v.tensor_tensor_scan(x_c, A_[:, 0, :], I_[:, t, :], 0.0, ALU.mult, ALU.add)); rd.wait()
                n = N_GATE + t
                dve.wait_ge(s_evac[n % 2], n // 2 + 1)
                v.tensor_tensor(H[:, t, :], H[:, t, :], x_c, ALU.mult).then_inc(s_yr, 1)
            dve.wait_ge(s_yr, 4)
            tr = Tally(dve, s_tr)
            an, kk = AN[64:128, 0, :], AN[64:128, 1, :]
            inv, turn, phase = (VC[64:128, VEC["trig"] + q:VEC["trig"] + q + 1] for q in range(3))
            dve.wait_ge(s_pos, 16)
            tr(v.tensor_copy(an, Q_[64:128, 0, :].bitcast(I32))); tr.wait()
            tr(v.tensor_scalar(an, an, inv, None, ALU.mult)); tr.wait()
            tr(v.tensor_scalar(kk, an, 1.0 / (2 * np.pi), turn, ALU.mult, ALU.add)); tr.wait()
            tr(v.tensor_scalar(kk, kk, 12582912.0, None, ALU.add)); tr.wait()
            tr(v.tensor_scalar(kk, kk, -12582912.0, None, ALU.add)); tr.wait()
            for c in TWO_PI_PARTS:
                tr(v.scalar_tensor_tensor(out=an, in0=kk, scalar=-c, in1=an, op0=ALU.mult, op1=ALU.add)); tr.wait()
            tr(v.tensor_scalar(an, an, phase, None, ALU.add)); tr.wait()
            tr(v.tensor_scalar(an, an, 3.14159, -3.14159, ALU.min, ALU.max)); tr.wait()
            tr(v.memset(V_[:, :, :, 64:128], 1.0))
            tr(v.memset(K_[96:97, :, :], 1.0))
            lat = Tally(dve, s_lat)
            for j in range(3):
                dve.wait_ge(s_rs, 2 + 2 * (j // 2))
                lat(v.scalar_tensor_tensor(out=CQ[:, j, :], in0=CQ[:, j, :], scalar=col("qn", j) if j < 2 else col("kvn"),
                                           in1=Q_[:, j // 2, :], op0=ALU.mult, op1=ALU.mult)); lat.wait()
                dve.wait_ge(s_lhi, j + 1)
                hi, lo = (CQH[:, j, :], CQL[:, j, :]) if j < 2 else (CKH[:, :], CKL[:, :])
                v.tensor_tensor(lo, CQ[:, j, :], hi.bitcast(F32), ALU.subtract).then_inc(s_llo, 1)
            dve.wait_ge(s_slab, N_HEADS)
            dve.wait_ge(s_sin, 1)
            v.tensor_tensor(K_[64:96, 0, :], PS[64:96, 0:2, :].rearrange("p b t -> p (b t)"), TRIG[64:96, :], ALU.mult).then_inc(s_kr, 1)
            v.tensor_tensor(K_[64:96, 1, :], PS[96:128, 0:2, :].rearrange("p b t -> p (b t)"), TRIG[96:128, :], ALU.mult).then_inc(s_evac[0], 1)
            dve.wait_ge(s_kr, 1)
            dve.wait_ge(s_evac[0], 9)
            v.tensor_tensor(K_[64:96, 0, :], K_[64:96, 0, :], K_[64:96, 1, :], ALU.add).then_inc(s_kr, 1)
            dve.wait_ge(s_kr, 2)
            v.tensor_copy(K_[64:96, 1, :], K_[64:96, 0, :]).then_inc(s_kr, 1)
            dve.wait_ge(s_kr, 3)
            rope, mx, yt = Tally(dve, s_rope), Tally(dve, s_mx), Tally(dve, s_y)
            def turn(i, u):
                dve.wait_ge(s_hp, 4 * i + (2 * u + 1))
                rope(v.tensor_tensor(RT[64:96, 0, :], flat(0)[64:96, :], TRIG[64:96, :], ALU.mult))
                rope(v.tensor_tensor(RT[64:96, 1, :], flat(0)[96:128, :], TRIG[96:128, :], ALU.mult)); rope.wait()
                rope(v.tensor_tensor(Q_[64:96, u % 2, :], RT[64:96, 0, :], RT[64:96, 1, :], ALU.add))

            def reduce(i, u, j):
                dve.wait_ge(s_s, 16 * i + (8 * u + j + 1))
                v.tensor_reduce(MX[:, u % 2, j:j + 1], flat(j % 2)[:, 0:(j + 1) * P], AX.X, ALU.max).then_inc(s_mx, 1)

            def negate(i, u):
                dve.wait_ge(s_row, 2 * i + (u + 1))
                v.tensor_scalar(Q_[96:97, u % 2, :], flat(0)[0:1, :], -1.0, None, ALU.mult).then_inc(s_neg, 1)

            def finish(i, u, hf):
                o = slice(64 * u, 64 * u + 64)
                dve.wait_ge(s_pv, 24 * i + (12 * u + (4 if hf == 0 else 12)))
                yt(v.reciprocal(RC[o, 0, :], PS[64:128, 4 + hf, :])); yt.wait()
                yt(v.tensor_tensor(RC[o, 1, :], PS[0:64, 4 + hf, :], RC[o, 0, :], ALU.mult)); yt.wait()
                g = H[o, bass.ds(i + 4, 1), hf * HB:(hf + 1) * HB].rearrange("p o t -> p (o t)")
                ins = v.tensor_tensor(g, g, RC[o, 1, :], ALU.mult)
                if hf == 0:
                    yt(ins)
                else:
                    ins.then_inc(s_evac[(N_HEADS + u) % 2], 1)

            def head(i, u, following):
                if following:
                    turn(i, u + 1)
                    for j in range(3):
                        reduce(i, u + 1, j)
                finish(i, u, 0)
                if following:
                    for j in range(3, KT):
                        reduce(i, u + 1, j)
                    negate(i, u + 1)
                finish(i, u, 1)

            v.memset(MX[:, :, :], 0.0).then_inc(s_y, 5)
            yt.n = 5
            turn(0, 0)
            for j in range(KT):
                reduce(0, 0, j)
            negate(0, 0)
            with dve.Fori(0, MLA_H // 2 - 1) as i:
                rope.loop(i, 6), yt.loop(i, 10)
                for u in range(2):
                    head(i, u, True)
            rope.end(MLA_H // 2 - 1), yt.end(MLA_H // 2 - 1)
            head(MLA_H // 2 - 1, 0, True)
            head(MLA_H // 2 - 1, 1, False)
            for k in range(KT):
                dve.wait_ge(s_yhi, k + 1)
                v.tensor_tensor(XL[:, k, :], H[:, k, :], XH_f[:, k, :], ALU.subtract).then_inc(s_ylo, 1)
            def total_up(c, total, k, n):
                if k:
                    dve.wait_ge(s_evac[n % 2], n // 2 + 1)
                    if k > 1:
                        c.wait()
                    c(v.tensor_tensor(total, H[:, 0, :] if k == 1 else total, H[:, k, :], ALU.add))

            centre1 = Tally(dve, ln1["c"].sem, ln1["c"].base)
            for k in range(KT):
                n = N_OUT_A + k
                dve.wait_ge(s_slab, n + 1)
                dve.wait_ge(s_xr[k % 2], 16 * (k // 2 + 1))
                v.scalar_tensor_tensor(out=H[:, k, :], in0=XR[:, k % 2, :], scalar=ALPHA, in1=flat(n % 2),
                                       op0=ALU.mult, op1=ALU.add).then_inc(s_evac[n % 2], 1)
                total_up(centre1, MU[:, :], k, n)

            def norm_dve(s, gain, center=None, split=True, keep=False, store=False):
                t = Tally(dve, s["t"].sem, s["t"].base)
                if center:
                    c = center
                    s["cs"].wait(dve, 1)
                    c(v.tensor_scalar(MU[:, :], flat(2), 1.0 / D, None, ALU.mult)); c.wait()
                    for k in range(KT):
                        c(v.tensor_tensor(H[:, k, :], H[:, k, :], MU[:, :], ALU.subtract))
                s["rs"].wait(dve, 1)

                def low(k):
                    s["hi"].wait(dve, k + 1)
                    src = H[:, k, :] if keep else TN[:, k % 2, :]
                    v.tensor_tensor(XL[:, k, :], src, XH_f[:, k, :], ALU.subtract).then_inc(s["lo"].sem, 1)

                for k in range(KT):
                    if k >= 2 and store:
                        dve.wait_ge(s_st_out[k % 2], 16 * (k // 2))
                    elif k >= 2:
                        s["lo" if split else "h"].wait(dve, k - 1)
                    t(v.scalar_tensor_tensor(out=TN[:, k % 2, :], in0=H[:, k, :], scalar=col(gain, k), in1=RS[:, :],
                                             op0=ALU.mult, op1=ALU.mult))
                    if k and split:
                        low(k - 1)
                if split:
                    low(KT - 1)

            norm_dve(ln1, "ln1_g", center=centre1, keep=True)
            dt = Tally(dve, s_dt)
            dve.wait_ge(s_dtt, 1)
            dt(v.tensor_tensor(DT, PS[:, 7, 0:256].rearrange("p (c h) -> p c h", h=SSD_HEADS),
                               RW[:, 0:32].unsqueeze(1).to_broadcast([P, CHUNKS, SSD_HEADS]), ALU.add)); dt.wait()
            e_, s_, s2_, t_ = (AV[:, 2 * q:2 * q + 2, :].rearrange("p a b -> p (a b)") for q in range(4))
            dt(v.tensor_copy(DTS[:, 5, :], DTS[:, 0, :])); dt.wait()
            dve.wait_ge(s_dta, 2)
            log1p_steps(s2_, e_, s_, s2_, t_, dt)
            dt(v.tensor_scalar(DTS[:, 0, :], DTS[:, 5, :], 0.0, None, ALU.max)); dt.wait()
            dt(v.tensor_tensor(DTS[:, 0, :], DTS[:, 0, :], s2_, ALU.add)); dt.wait()
            dve.wait_ge(s_dta, 3)
            dt(v.scalar_tensor_tensor(out=ADT, in0=DT, scalar=-1.0, in1=RW[:, 64:96].unsqueeze(1).to_broadcast([P, CHUNKS, SSD_HEADS]),
                                      op0=ALU.mult, op1=ALU.mult))
            assert dt.n == DT_STEPS, dt.n
            a_t, b_t, c_t = Tally(dve, s_a), Tally(dve, s_b), Tally(dve, s_c)
            cv = Tally(dve, s_cv)
            def group(g):
                def heads(x, c):
                    return x[:, c, bass.ds(g * HPG, HPG)].unsqueeze(2).to_broadcast([P, HPG, PDIM])

                def by_head(x):
                    return x.rearrange("p (h d) -> p h d", d=PDIM)

                def rates(c):
                    v.tensor_tensor(AV[:, :, :], CN[:, C_UPTO, :].unsqueeze(1).to_broadcast([P, HPG, P]),
                                    ADT[:, c, bass.ds(g * HPG, HPG)].unsqueeze(2).to_broadcast([P, HPG, P]), ALU.mult).then_inc(s_av, 1)

                cv(v.memset(ST[:, :], 0.0)); cv.wait()
                for step in range(CHUNKS + 2):
                    c = step
                    if c < CHUNKS:
                        if c == 0:
                            dve.wait_ge(s_cs, 6 * g + 6)
                            rates(0)
                        dve.wait_ge(s_cb, 8 * g + (c + 1))
                        dve.wait_ge(s_bk, 8 * g + (c + 1))
                        if c:
                            dve.wait_ge(s_m, 8 * g + c)
                        a_t(v.tensor_tensor(CB[:, :], PS[:, 4, 0:P], CN[:, C_UPTO, :], ALU.mult))
                        if c >= 2:
                            dve.wait_ge(s_core, 8 * g + (c - 1))
                        a_t(v.tensor_tensor(by_head(XF[:, c % 2, :]), by_head(PS[:, 5, :]), heads(DT, c), ALU.mult)); a_t.wait()
                        a_t(v.tensor_tensor(by_head(XFD[:, c % 2, :]), by_head(XF[:, c % 2, :]), heads(DS, c), ALU.mult)); a_t.wait()
                        if c + 1 < CHUNKS:
                            dve.wait_ge(s_seg, 8 * g + (c + 1))
                            rates(c + 1)
                    c = step - 1
                    if 0 <= c < CHUNKS:
                        dve.wait_ge(s_core, 8 * g + (c + 1))
                        b_t(v.tensor_tensor(by_head(ST[:, :]), by_head(ST[:, :]), heads(DEC, c), ALU.mult)); b_t.wait()
                        b_t(v.tensor_tensor(ST[:, :], ST[:, :], PS[:, 4, :], ALU.add)); b_t.wait()
                    c = step - 2
                    if 0 <= c < CHUNKS:
                        dve.wait_ge(s_yt, 8 * g + (c + 1))
                        for m in range(4):
                            x_c = XS[:, m, c * P:(c + 1) * P]
                            c_t(v.scalar_tensor_tensor(out=x_c, in0=x_c, scalar=VC[:, bass.ds(g * 4 + (VEC["ssd_d"] + m), 1)],
                                                       in1=PS[:, 5, m * P:(m + 1) * P], op0=ALU.mult, op1=ALU.add))
                    c = step - 1
                    if 0 <= c < CHUNKS:
                        b_t(v.tensor_tensor(by_head(YR[:, 0, :]), by_head(PS[:, 3, :]), heads(ECS, c), ALU.mult)); b_t.wait()
                        b_t(v.tensor_tensor(YR[:, 1, :], YR[:, 0, :], PS[:, 2, :], ALU.add))
                    c = step
                    if c < CHUNKS:
                        dve.wait_ge(s_ex, 8 * g + (c + 1))
                        v.tensor_tensor(E[:, c % 2, :, :], E[:, c % 2, :, :], CB[:, :].unsqueeze(1).to_broadcast([P, HPG, P]),
                                        ALU.mult).then_inc(s_m, 1)
                c_t.wait()
                for m in range(4):
                    if m == 0:
                        dve.wait_ge(s_evac[(N_CORE - 1) % 2], (SSD_SLABS // 2) * g + (N_CORE - 1) // 2 + 1)
                    else:
                        dve.wait_ge(s_zs, 3 * g + m)
                    v.tensor_tensor(XS[:, m, :], XS[:, m, :], Z[:, m, :], ALU.mult).then_inc(s_g, 1)
                rs = E[:, 0, :, :].rearrange("p h l -> p (h l)")
                dve.wait_ge(s_gr, g + 1)
                for m in range(5):
                    if m < 4:
                        if m >= 2:
                            dve.wait_ge(s_gl, 4 * g + (m - 1))
                        v.scalar_tensor_tensor(out=CV[:, m % 2, :], in0=XS[:, m, :], scalar=VC[:, bass.ds(g * 4 + (VEC["ssd_n"] + m), 1)],
                                               in1=rs, op0=ALU.mult, op1=ALU.mult).then_inc(s_gt, 1)
                    if m:
                        dve.wait_ge(s_gh, 4 * g + m)
                        v.tensor_tensor(YL[:, m - 1, :], CV[:, (m - 1) % 2, :], YH[:, m - 1, :].bitcast(F32), ALU.subtract).then_inc(s_gl, 1)

            def conv_tile(n, q, g, cg):
                dve.wait_ge(s_slab, SSD_SLABS * g + (n + 1))
                if q >= 2:
                    dve.wait_ge(s_cs, 6 * cg + (q - 1))
                src, y = flat(n % 2), CV[:, q % 2, :]

                def wcol(tap):
                    return VC[:, bass.ds(cg * 24 + (VEC["sc_w"] + 4 * q + tap), 1)]

                cv(v.tensor_scalar(y, src, wcol(3), VC[:, bass.ds(cg * 6 + (VEC["sc_b"] + q), 1)], ALU.mult, ALU.add)); cv.wait()
                for d in (1, 2, 3):
                    ins = v.scalar_tensor_tensor(out=y[:, d:TOK], in0=src[:, 0:TOK - d], scalar=wcol(3 - d),
                                                 in1=y[:, d:TOK], op0=ALU.mult, op1=ALU.add)
                    if d < 3:
                        cv(ins)
                        cv.wait()
                    else:
                        ins.then_inc(s_evac[n % 2], 1)

            def out_tiles(n0, g, centre=None):
                for q in range(4):
                    n = n0 + q
                    dve.wait_ge(s_oh, 4 * g + (q + 1))
                    v.tensor_tensor(H[:, 2 * q, :], H[:, 2 * q, :], flat(2), ALU.add).then_inc(s_oe, 1)
                    dve.wait_ge(s_slab, SSD_SLABS * g + (n + 1))
                    v.tensor_tensor(H[:, 2 * q + 1, :], H[:, 2 * q + 1, :], flat(3), ALU.add).then_inc(s_evac[n % 2], 1)
                    if centre:
                        done = (SSD_SLABS // 2) * g + n // 2 + 1
                        for k in (2 * q, 2 * q + 1):
                            if k:
                                dve.wait_ge(s_oe, 4 * g + (q + 1))
                                dve.wait_ge(s_evac[n % 2], done)
                                if k > 1:
                                    centre.wait()
                                centre(v.tensor_tensor(SUM2, H[:, 0, :] if k == 1 else SUM2, H[:, k, :], ALU.add))

            for q in range(6):
                conv_tile(N_SSD + q, q, 0, 0)
                if q >= 2:
                    for k in (2 * q - 4, 2 * q - 3):
                        dt(v.tensor_scalar(H[:, k, :], H[:, k, :], ALPHA, None, ALU.mult))
            dt.wait()
            dve.wait_ge(s_dta, 5)
            with dve.Fori(0, GROUPS - 1) as g:
                a_t.loop(g, 24), b_t.loop(g, 32), c_t.loop(g, 32), cv.loop(g, 19)
                group(g)
                dve.wait_ge(s_gl, 4 * g + 4)
                for q in range(2):
                    conv_tile(N_CORE + 3 + q, q, g, g + 1)
                out_tiles(N_CORE + 5, g)
                for q in range(2, 6):
                    conv_tile(N_CORE + 7 + q, q, g, g + 1)
            for tally in (a_t, b_t, c_t, cv):
                tally.end(GROUPS - 1)
            group(GROUPS - 1)
            centre2 = Tally(dve, ln2["c"].sem, ln2["c"].base)
            out_tiles(N_CORE + 3, GROUPS - 1, centre2)
            norm_dve(ln2, "ln2_g", center=centre2, split=False, keep=True)
            norm_dve(mix, "g_mix")
            cc = Tally(dve, s_cc)
            for m in range(4):
                n = N_IN2 + 3 * m
                y = CONV[:, m, :]
                dve.wait_ge(s_evac[n % 2], n // 2 + 1)
                dve.wait_ge(s_slab, n + 2)
                cc(v.tensor_tensor(CU, flat((n + 1) % 2), CC, ALU.mult)); cc.wait()
                v.tensor_scalar(y, CU, col("c2_w", 8 + m), None, ALU.mult).then_inc(s_evac[(n + 1) % 2], 1)
                dve.wait_ge(s_evac[(n + 1) % 2], (n + 1) // 2 + 1)
                for d in (1, 2):
                    cc(v.scalar_tensor_tensor(out=y[:, d:TOK], in0=CU[:, 0:TOK - d], scalar=col("c2_w", 4 * (2 - d) + m),
                                              in1=y[:, d:TOK], op0=ALU.mult, op1=ALU.add)); cc.wait()
                dve.wait_ge(s_slab, n + 3)
                v.tensor_tensor(y, flat(n % 2), y, ALU.mult).then_inc(s_evac[n % 2], 1)
                dve.wait_ge(s_evac[n % 2], n // 2 + 2)
                cc(v.memset(SM[:, 3, 0:1], 0.0))
            dg = Tally(dve, s_dg)
            v.memset(SM[:, 4, 0:1], 0.0).then_inc(s_at, 1)
            v.memset(SM[:, 5, 0:1], 0.0).then_inc(s_fe, 1)
            with dve.Fori(0, 2) as i:
                dg.loop(i, 32)
                for mm_ in range(2):
                    def at(per, k):
                        return (2 * per) * i + (per * mm_ + k)

                    def over_heads(c):
                        return CN[:, c, :].unsqueeze(1).to_broadcast([P, 2, P])

                    for step in range(NU + 1):
                        t = step
                        if t < NU:
                            hf, j = SB_UNITS[t]
                            q0 = max(0, j * P - hf * HB)
                            z, l = pair(3 * (t % 2))[:, :, q0:HB], SB_L[:, t % 2, :, q0:HB]
                            sp, ls = SB_P[:, t % 3, :, :], SB_A[:, t % 3, :, :]
                            dve.wait_ge(s_al, at(3 * NU, 3 * t + 3))
                            if t >= 3:
                                dve.wait_ge(s_o, at(NU, t - 2))
                            ins = v.scalar_tensor_tensor(out=sp[:, :, q0:HB], in0=z, scalar=0.0, in1=l, op0=ALU.max, op1=ALU.add)
                            if j >= 4 * hf:
                                dg(ins); dg.wait()
                                v.tensor_tensor(ls[:, :, q0:HB], z, sp[:, :, q0:HB], ALU.subtract).then_inc(s_ls, 1)
                                dve.wait_ge(s_ls, at(NU, t + 1))
                                v.tensor_tensor(sp[:, :, q0:q0 + P], sp[:, :, q0:q0 + P], over_heads(C_NOTLATER), ALU.mult).then_inc(s_sp, 1)
                                dg(v.tensor_tensor(ls[:, :, q0:q0 + P], ls[:, :, q0:q0 + P], over_heads(C_NEGS), ALU.add)); dg.wait()
                            else:
                                ins.then_inc(s_sp, 1)
                                dve.wait_ge(s_sp, at(NU, t + 1))
                                v.tensor_tensor(ls[:, :, q0:HB], z, sp[:, :, q0:HB], ALU.subtract).then_inc(s_ls, 1)
                                dve.wait_ge(s_ls, at(NU, t + 1))
                        t = step - 1
                        if t >= 0:
                            hf, j = SB_UNITS[t]
                            q0 = max(0, j * P - hf * HB)
                            ls = SB_A[:, t % 3, :, q0:HB]
                            dve.wait_ge(s_su, at(NU, t + 1))
                            v.tensor_tensor(ls, ls, PS[:, 2:4, q0:HB], ALU.subtract).then_inc(s_d, 1)
                            if j == 0:
                                dve.wait_ge(s_o, at(NU, t + 1))
                                for u in range(2):
                                    a = ATT[64 * u:64 * u + 64, bass.ds(2 * i + mm_, 1), hf * HB:(hf + 1) * HB].rearrange("p o t -> p (o t)")
                                    v.tensor_copy(a, PS[0:64, 4 + u, :]).then_inc(s_at, 1)
            dg.end(2)
            for k in range(9):
                if k < 8:
                    dve.wait_ge(s_hr, k + 1)
                    if k >= 2:
                        dve.wait_ge(s_hl, k - 1)
                    src = CONV[:, k, :] if k < 4 else ATT[:, k - 4, :]
                    v.scalar_tensor_tensor(out=HT[:, k % 2, :], in0=src, scalar=col("g_co", k), in1=HR[:, k % 2, :],
                                           op0=ALU.mult, op1=ALU.mult).then_inc(s_ht, 1)
                if k:
                    dve.wait_ge(s_hh, k)
                    v.tensor_tensor(XL[:, k - 1, :], HT[:, (k - 1) % 2, :], XH_f[:, k - 1, :], ALU.subtract).then_inc(s_hl, 1)
            for k in range(KT):
                n = N_OUT2 + k
                dve.wait_ge(s_slab, n + 1)
                v.tensor_tensor(H[:, k, :], H[:, k, :], flat(n % 2), ALU.add).then_inc(s_evac[n % 2], 1)
            norm_dve(mlp, "g_mlp")

            def up_tile(b, q, n, half, cnt):
                dve.wait_ge(s_evac[n % 2], half + n // 2 + 1)
                v.tensor_tensor(FT[:, q % 2, :], FT[:, q % 2, :], FT[:, q % 2, :], ALU.mult).then_inc(s_ff, 1)
                dve.wait_ge(s_fh, cnt + q + 1)
                v.tensor_tensor(UL[:, b % 2, q, :], FT[:, q % 2, :], UH[:, b % 2, q, :].bitcast(F32), ALU.subtract).then_inc(s_fl, 1)

            def down_tiles(n, dyn, done, q):
                dve.wait_ge(s_fo, 4 * done + (q + 1))
                v.tensor_tensor(H[:, 2 * q, :], H[:, 2 * q, :], flat(2), ALU.add).then_inc(s_fe, 1)
                dve.wait_ge(s_slab, 2 * dyn + (n + 1))
                v.tensor_tensor(H[:, 2 * q + 1, :], H[:, 2 * q + 1, :], flat(3), ALU.add).then_inc(s_evac[n % 2], 1)

            for q in range(4):
                up_tile(0, q, N_FFN + q, 0, 0)
            with dve.Fori(0, 3) as i:
                for e in range(2):
                    for q in range(4):
                        up_tile(1 + e, q, N_FFN + 4 + 8 * e + q, 8 * i, 8 * i + 4 * (1 + e))
                    for q in range(4):
                        down_tiles(N_FFN + 8 + 8 * e + q, 8 * i, 2 * i + e, q)
            for q in range(4):
                up_tile(7, q, N_FFN + 52 + q, 0, 28)
            for b in (6, 7):
                for q in range(4):
                    down_tiles(N_FFN + 56 + 4 * (b - 6) + q, 0, b, q)
            dve.wait_ge(s_evac[(N_PLE - 1) % 2], (N_PLE - 1) // 2 + 1)
            dve.wait_ge(s_fe, 33)
            for k in range(2):
                dve.wait_ge(s_ph, k + 1)
                v.tensor_tensor(PL[:, k, :], XR[:, k, :], PH[:, k, :].bitcast(F32), ALU.subtract).then_inc(s_pw, 1)
            norm_dve(ple, "g_ple")
            for k in range(KT):
                n = N_PLE + 2 + k
                dve.wait_ge(s_evac[n % 2], n // 2 + 1)
                v.tensor_tensor(XR[:, k % 2, :], XR[:, k % 2, :], PJ[:, k, :], ALU.mult).then_inc(s_sg, 1)
                dve.wait_ge(s_sg, k + 1)
                v.tensor_tensor(H[:, k, :], H[:, k, :], XR[:, k % 2, :], ALU.add).then_inc(s_h3, 1)
            dve.wait_ge(s_h3, KT)
            norm_dve(fin, "g_fin", split=False, store=True)
    return nc


def _layout(inputs):
    f = {k: np.asarray(a) for k, a in inputs.items()}

    def cols(a):
        return a.reshape(-1, P).T

    def slabs(wm, kt):
        K, M = wm.shape
        per = 8 // kt
        a = wm.reshape(K // P // kt, kt, P, M // P // per, per, P)
        return a.transpose(0, 3, 2, 4, 1, 5).reshape(-1, P, 1024)

    def pad(wm, n):
        return np.concatenate([wm, np.zeros((wm.shape[0], n - wm.shape[1]), wm.dtype)], 1)

    out = []
    wa = f["ab_w_in"][0]
    out.append(slabs(wa[:, 0:512], 8))
    bd = np.zeros((P, 8, P), np.float32)
    for g, nm in enumerate(("ab_gate_a_w", "ab_gate_x_w")):
        for h in range(8):
            o = 64 * (h % 2)
            bd[o:o + 64, 4 * g + h // 2, o:o + 64] = f[nm][0, h]
    out.append(bd.reshape(1, P, 1024))
    out.append(slabs(wa[:, 512:1536], 8))
    out.append(slabs(wa[:, 1536:1792], 8))
    out.append(slabs(wa[:, 1792:1920], 8))
    kr = wa[:, 1920:1952]
    krs = np.concatenate([np.zeros((D, 64), np.float32), kr, kr[:, 16:], kr[:, :16]], 1)
    out.append(slabs(krs, 8))
    uq = f["mla_w_uq"][0].reshape(2, P, MLA_H, 96)
    ukv = f["mla_w_ukv"][0].reshape(P, MLA_H, 128)
    for h in range(MLA_H):
        s = np.zeros((P, 8, P), np.float32)
        for k in range(2):
            s[:, k, 0:96] = uq[k, :, h]
            s[:, k, 96:112] = uq[k, :, h, 80:96]
            s[:, k, 112:128] = uq[k, :, h, 64:80]
        s[:, 2] = ukv[:, h]
        out.append(s.reshape(1, P, 1024))
    out.append(slabs(f["ab_w_out"][0], 8))
    ws = f["ssd_w_in"][0]
    out.append(slabs(pad(ws[:, 5120:5152], 128), 8))
    part = {}
    for g in range(GROUPS):
        part["b", g] = slabs(ws[:, 4096 + 128 * g:4096 + 128 * g + 128], 8)
        part["c", g] = slabs(ws[:, 4608 + 128 * g:4608 + 128 * g + 128], 8)
        part["x", g] = slabs(ws[:, 2048 + 512 * g:2048 + 512 * g + 512], 8)
        z = slabs(ws[:, 512 * g:512 * g + 512], 8)
        part["z0", g], part["z", g] = z[:1], z[1:]
        part["out", g] = slabs(f["ssd_w_out"][0][512 * g:512 * g + 512], 4)
    out += [part[k, 0] for k in ("b", "c", "x", "z0")]
    for g in range(GROUPS):
        out.append(part["z", g])
        if g < GROUPS - 1:
            out += [part["b", g + 1], part["c", g + 1], part["out", g], part["x", g + 1], part["z0", g + 1]]
        else:
            out.append(part["out", g])
    w2 = f["w_in_2"][0]
    for m in range(4):
        for o in (512, 1024, 0):
            out.append(slabs(w2[:, o + 128 * m:o + 128 * m + 128], 8))
    for m in range(4):
        for o in (1536, 2048, 2560):
            out.append(slabs(w2[:, o + 128 * m:o + 128 * m + 128], 8))
    out.append(slabs(f["w_out_2"][0], 8))
    up, down = f["w_up_2"][0], f["w_down_2"][0]
    for b in range(FFN_BLOCKS + 1):
        if b < FFN_BLOCKS:
            out.append(slabs(up[:, 512 * b:512 * b + 512], 8))
        if b:
            out.append(slabs(down[512 * (b - 1):512 * b], 4))
    out.append(slabs(f["w_ple_proj_2"][0], 2))
    out.append(slabs(f["w_ple_gate_2"][0], 8))
    wall = np.ascontiguousarray(np.concatenate(out, 0))
    assert wall.shape[0] == NSLAB, (wall.shape, NSLAB)

    ang = np.arange(P)
    inv = np.float32(10000.0) ** (-np.arange(0, 32, 2, dtype=np.float32) / np.float32(32))
    trig = np.zeros((P, 3), np.float32)
    trig[:, 0] = inv[ang % 16]
    turn = np.where(ang < 96, 0.25, np.where(ang < 112, 0.5, 0.0))
    trig[:, 1] = turn
    trig[:, 2] = turn * 2 * np.pi
    sc = f["ssd_conv_w"][0]
    scb = f["ssd_conv_b"][0]

    def group_order(a):
        return np.concatenate([np.concatenate([a[..., 2048 + 128 * g:2176 + 128 * g], a[..., 2560 + 128 * g:2688 + 128 * g],
                                               a[..., 512 * g:512 * g + 512]], -1) for g in range(GROUPS)], -1)

    sc_t = group_order(sc).reshape(4, 24, P).transpose(2, 1, 0).reshape(P, 96)
    parts = [cols(f["ab_conv_w"][0]), cols(f["ab_conv_b"][0]), cols(f["ab_gate_a_b"][0]), cols(f["ab_gate_x_b"][0]),
             cols(f["ab_lambda"][0]), cols(f["mla_q_norm"][0]), cols(f["mla_kv_norm"][0]), cols(f["ab_ln_g"][0]),
             cols(f["ab_ln_b"][0]), sc_t, cols(group_order(scb)), cols(np.repeat(f["ssd_d"][0], 64)), cols(f["ssd_norm"][0]),
             cols(f["ssd_ln_g"][0]), cols(f["ssd_ln_b"][0]), cols(f["g_mix_2"][0]), cols(f["conv_w_2"][0]),
             cols(f["g_conv_out_2"][0]), cols(f["g_attn_out_2"][0]), cols(f["g_mlp_2"][0]), cols(f["g_ple_2"][0]),
             cols(f["g_final_2"]), trig]
    vec = np.ascontiguousarray(np.concatenate(parts, 1))
    assert vec.shape == (P, NVEC), vec.shape
    rows = np.ascontiguousarray(np.broadcast_to(
        np.concatenate([f["ssd_dt_bias"][0], f["ssd_a_log"][0], f["ssd_d"][0]])[None], (P, 96)))
    a, b = np.arange(P)[:, None], np.arange(P)[None, :]
    c = np.zeros((P, NCONST, P), np.float32)
    c[:, C_ID] = a == b
    c[:, C_AFTER] = a > b
    c[:, C_UPTO] = a <= b
    c[:, C_ONES] = 1
    c[:, C_BLK] = (a // 64) == (b // 64)
    c[:, C_NEGQ] = np.where(b <= a, 0, NEG)
    c[:, C_NEGK] = np.where(a <= b, 0, NEG)
    c[:, C_NOTLATER] = a < b
    c[:, C_NEGS] = np.where(a < b, 0, NEG)
    return {
        "x_t": np.ascontiguousarray(f["x"][0].T.reshape(KT, P, TOK)),
        "pos": np.ascontiguousarray(f["positions"].reshape(1, TOK)),
        "w": wall, "vec": vec, "rows": rows, "consts": c,
        "p_t": np.ascontiguousarray(f["p_2"][0, 0].T.reshape(2, P, TOK)),
    }


def build(nc, arrays):
    args = [nc.dram_tensor(k, a.shape, mybir.dt.from_np(a.dtype), kind="ExternalInput").ap() for k, a in arrays.items()]
    out = nc.dram_tensor("out_t", (KT, P, TOK), F32, kind="ExternalOutput").ap()
    program(nc, *args, out)


def kernel(**inputs):
    import concourse.bacc as bacc
    from concourse.bass_utils import run_bass_kernel_spmd

    arrays = _layout(inputs)
    nc = bacc.Bacc("TRN2", target_bir_lowering=False, num_devices=1)
    build(nc, arrays)
    r = run_bass_kernel_spmd(nc, [arrays], core_ids=[0])
    o = r.results[0]["out_t"].reshape(D, TOK)
    return np.ascontiguousarray(o.T).reshape(1, TOK, D)
```
